# Optimizing a Trainium2 kernel written in Bass

```python
import jax, jax.numpy as jnp
from jax import lax
import numpy as np

D_MODEL = 1024
BATCH = 1
SEQ = 256
DEPTH = 1

N_MIXERS = 4
MIX_WIDTH = D_MODEL // 4
HEAD_DIM = 64
N_HEADS = MIX_WIDTH // HEAD_DIM
CHUNK = 64
ROPE_THETA = 10000.0
NORM_EPS = 1e-6
NEG_INF = -1e30

CONV_W = 4
NSA_KV_GROUPS = 2
NSA_HPG = N_HEADS // NSA_KV_GROUPS
KV_WIDTH = NSA_KV_GROUPS * HEAD_DIM
CMP_LEN = 32
CMP_STRIDE = 16
SEL_BLOCK = 64
SEL_TOPK = 16
WINDOW = 512
WIN_QBLOCK = 128
SEL_QBLOCK = 32
FORCE_BONUS = 1e3
PEER_HEADS = 8
PEER_NKEYS = 128
PEER_EXPERTS = PEER_NKEYS * PEER_NKEYS
PEER_QDIM = 256
PEER_TOPK = 16
PEER_TCHUNK = 128

IN_WIDTHS = (
    MIX_WIDTH, MIX_WIDTH, MIX_WIDTH, MIX_WIDTH,
    MIX_WIDTH, MIX_WIDTH, MIX_WIDTH, N_HEADS, N_HEADS, MIX_WIDTH,
    MIX_WIDTH, KV_WIDTH, KV_WIDTH, KV_WIDTH, KV_WIDTH, KV_WIDTH, KV_WIDTH, 3 * N_HEADS,
    MIX_WIDTH, MIX_WIDTH, MIX_WIDTH, MIX_WIDTH,
)
IN_OFFSETS = tuple(int(v) for v in np.cumsum(IN_WIDTHS)[:-1])
N_IN = sum(IN_WIDTHS)

kernel_name = 'hybrid_hgrn2_mlstm_nsa_retnet_peer'

def rms_norm(x, g):
    xf = x.astype(jnp.float32)
    y = xf * lax.rsqrt(jnp.mean(xf * xf, axis=-1, keepdims=True) + NORM_EPS)
    return (y * g.astype(jnp.float32)).astype(x.dtype)

def rope_tables(seq_len):
    inv = 1.0 / (ROPE_THETA ** (jnp.arange(0, HEAD_DIM, 2, dtype=jnp.float32) / HEAD_DIM))
    ang = jnp.arange(seq_len, dtype=jnp.float32)[:, None] * inv[None, :]
    return jnp.cos(ang), jnp.sin(ang)

def apply_rope(x, cos, sin):
    x1, x2 = jnp.split(x, 2, axis=-1)
    c = cos[None, :, None, :].astype(x.dtype)
    s = sin[None, :, None, :].astype(x.dtype)
    return jnp.concatenate([x1 * c - x2 * s, x1 * s + x2 * c], axis=-1)

def to_chunks(x):
    b, s, h, d = x.shape
    return x.reshape(b, s // CHUNK, CHUNK, h, d).transpose(1, 0, 3, 2, 4)

def from_chunks(y):
    n, b, h, c, d = y.shape
    return y.transpose(1, 0, 3, 2, 4).reshape(b, n * c, h, d)

def gate_chunks(g):
    b, s, h = g.shape
    return g.reshape(b, s // CHUNK, CHUNK, h).transpose(1, 0, 3, 2)

def masked_softmax(s, mask):
    s = jnp.where(mask, s.astype(jnp.float32), NEG_INF)
    return jnp.where(mask, jax.nn.softmax(s, axis=-1), 0.0)

def causal_dwconv(x, w, b):
    y = lax.conv_general_dilated(x, w[:, None, :].astype(x.dtype), window_strides=(1,),
                                 padding=[(w.shape[0] - 1, 0)],
                                 dimension_numbers=('NWC', 'WIO', 'NWC'),
                                 feature_group_count=x.shape[-1])
    return y + b.astype(x.dtype)

def hgrn2_mixer(q_pre, f_pre, i_pre, g_pre, lb, onorm_g):
    bsz, seq, _ = q_pre.shape
    heads = lambda t: t.reshape(bsz, seq, N_HEADS, HEAD_DIM).astype(jnp.float32)
    q = jax.nn.silu(heads(q_pre))
    fl = heads(f_pre)
    lbh = lb.reshape(N_HEADS, HEAD_DIM).astype(jnp.float32)
    log_f = jnp.logaddexp(jnp.log(lbh), jnp.log1p(-lbh) + jax.nn.log_sigmoid(fl))
    k = (1.0 - lbh) * jax.nn.sigmoid(-fl)
    v = heads(i_pre)
    causal = jnp.tril(jnp.ones((CHUNK, CHUNK), dtype=bool))[:, :, None]

    def step(state, xs):
        qc, kc, vc, gc = xs
        b = jnp.cumsum(gc, axis=2)
        diff = b[:, :, :, None, :] - b[:, :, None, :, :]
        decay = jnp.exp(jnp.where(causal, diff, -jnp.inf))
        a = jnp.einsum('bhtd,bhsd,bhtsd->bhts', qc, kc, decay)
        o = jnp.einsum('bhts,bhse->bhte', a, vc) + jnp.einsum('bhtd,bhde->bhte', qc * jnp.exp(b), state)
        b_last = b[:, :, -1:, :]
        state = jnp.exp(b_last[:, :, 0, :])[..., None] * state + \
            jnp.einsum('bhsd,bhse->bhde', kc * jnp.exp(b_last - b), vc)
        return state, o

    s0 = jnp.zeros((bsz, N_HEADS, HEAD_DIM, HEAD_DIM), jnp.float32)
    _, o = lax.scan(step, s0, (to_chunks(q), to_chunks(k), to_chunks(v), to_chunks(log_f)))
    o = rms_norm(from_chunks(o), onorm_g.reshape(N_HEADS, HEAD_DIM)) * jax.nn.silu(heads(g_pre))
    return o.reshape(bsz, seq, MIX_WIDTH).astype(q_pre.dtype)

def mlstm_mixer(q_pre, k_pre, v_pre, i_pre, f_pre, o_pre, conv_w, conv_b, gate_b, onorm_g):
    bsz, seq, _ = q_pre.shape
    heads = lambda t: t.reshape(bsz, seq, N_HEADS, HEAD_DIM).astype(jnp.float32)
    qk = jax.nn.silu(causal_dwconv(jnp.concatenate([q_pre, k_pre], axis=-1), conv_w, conv_b))
    q_c, k_c = jnp.split(qk, 2, axis=-1)
    q = heads(q_c)
    k = heads(k_c) * (HEAD_DIM ** -0.5)
    v = heads(v_pre)
    log_i = (i_pre + gate_b[:N_HEADS]).astype(jnp.float32)
    log_f = jax.nn.log_sigmoid((f_pre + gate_b[N_HEADS:]).astype(jnp.float32))
    causal = jnp.tril(jnp.ones((CHUNK, CHUNK), dtype=bool))

    def step(carry, xs):
        c_st, n_st, m_st = carry
        qc, kc, vc, li, lf = xs
        b = jnp.cumsum(lf, axis=-1)
        dmat = jnp.where(causal, b[..., :, None] - b[..., None, :] + li[..., None, :], -jnp.inf)
        inter = b + m_st[..., None]
        m = jnp.maximum(inter, jnp.max(dmat, axis=-1))
        w = jnp.exp(dmat - m[..., None]) * jnp.einsum('bhtd,bhsd->bhts', qc, kc)
        s_inter = jnp.exp(inter - m)
        num = s_inter[..., None] * jnp.einsum('bhtd,bhde->bhte', qc, c_st) + jnp.einsum('bhts,bhse->bhte', w, vc)
        den = s_inter * jnp.einsum('bhtd,bhd->bht', qc, n_st) + jnp.sum(w, axis=-1)
        h = num / jnp.maximum(jnp.abs(den), jnp.exp(-m))[..., None]
        b_last = b[..., -1]
        lw = b_last[..., None] - b + li
        m_new = jnp.maximum(b_last + m_st, jnp.max(lw, axis=-1))
        wk = jnp.exp(lw - m_new[..., None])
        decay = jnp.exp(b_last + m_st - m_new)
        c_new = decay[..., None, None] * c_st + jnp.einsum('bhs,bhsd,bhse->bhde', wk, kc, vc)
        n_new = decay[..., None] * n_st + jnp.einsum('bhs,bhsd->bhd', wk, kc)
        return (c_new, n_new, m_new), h

    init = (jnp.zeros((bsz, N_HEADS, HEAD_DIM, HEAD_DIM), jnp.float32),
            jnp.zeros((bsz, N_HEADS, HEAD_DIM), jnp.float32),
            jnp.zeros((bsz, N_HEADS), jnp.float32))
    _, h = lax.scan(step, init, (to_chunks(q), to_chunks(k), to_chunks(v), gate_chunks(log_i), gate_chunks(log_f)))
    h = rms_norm(from_chunks(h), onorm_g.reshape(N_HEADS, HEAD_DIM)) * jax.nn.sigmoid(heads(o_pre))
    return h.reshape(bsz, seq, MIX_WIDTH).astype(q_pre.dtype)

def nsa_mixer(q_pre, kc_pre, vc_pre, ks_pre, vs_pre, kw_pre, vw_pre, gate_pre, cos, sin,
              qnorm_g, knorm_g, cmp_pe, cmp_w):
    bsz, seq, _ = q_pre.shape
    G, HG, DH = NSA_KV_GROUPS, NSA_HPG, HEAD_DIM
    scale = DH ** -0.5
    kvh = lambda t: t.reshape(bsz, seq, G, DH)
    q = rms_norm(q_pre.reshape(bsz, seq, N_HEADS, DH), qnorm_g)
    q_cmp = q.reshape(bsz, seq, G, HG, DH)
    q_rot = apply_rope(q, cos, sin).reshape(bsz, seq, G, HG, DH)
    pos = jnp.arange(seq)

    n_cmp = (seq - CMP_LEN) // CMP_STRIDE + 1
    cmp_start = jnp.arange(n_cmp) * CMP_STRIDE
    cidx = cmp_start[:, None] + jnp.arange(CMP_LEN)[None, :]

    def compress(t, pe, w):
        blocks = t[:, cidx] + pe[None, None, :, None, :].astype(t.dtype)
        return jnp.einsum('bnlgd,lde->bnge', blocks, w.reshape(CMP_LEN, DH, DH))

    k_cmp = rms_norm(compress(kvh(kc_pre), cmp_pe[0], cmp_w[0]), knorm_g[0])
    v_cmp = compress(kvh(vc_pre), cmp_pe[1], cmp_w[1])
    s_cmp = jnp.einsum('bsghd,bngd->bghsn', q_cmp, k_cmp).astype(jnp.float32) * scale
    cmp_mask = (cmp_start + CMP_LEN - 1)[None, :] <= pos[:, None]
    p_cmp = masked_softmax(s_cmp, cmp_mask)
    o_cmp = jnp.einsum('bghsn,bngd->bsghd', p_cmp, v_cmp)

    n_sel = seq // SEL_BLOCK
    n_top = min(SEL_TOPK, n_sel)
    sel_start = jnp.arange(n_sel) * SEL_BLOCK
    overlap = ((cmp_start[:, None] < sel_start[None, :] + SEL_BLOCK) &
               (cmp_start[:, None] + CMP_LEN > sel_start[None, :])).astype(jnp.float32)
    imp = jnp.einsum('bghsn,nj->bgsj', p_cmp, overlap)
    blk = jnp.arange(n_sel)[None, :]
    cur = (pos // SEL_BLOCK)[:, None]
    forced = (blk == 0) | (blk == cur) | (blk == cur - 1)
    imp = jnp.where(blk <= cur, imp + FORCE_BONUS * forced.astype(jnp.float32), NEG_INF)
    top_val, sel_idx = lax.top_k(imp, n_top)
    sel_ok = top_val > 0.5 * NEG_INF

    k_sel = apply_rope(rms_norm(kvh(ks_pre), knorm_g[1]), cos, sin)
    k_blocks = k_sel.reshape(bsz, n_sel, SEL_BLOCK, G, DH).transpose(0, 3, 1, 2, 4)
    v_blocks = kvh(vs_pre).reshape(bsz, n_sel, SEL_BLOCK, G, DH).transpose(0, 3, 1, 2, 4)
    nqb = seq // SEL_QBLOCK
    q_b = q_rot.reshape(bsz, nqb, SEL_QBLOCK, G, HG, DH).transpose(1, 0, 2, 3, 4, 5)
    idx_b = sel_idx.reshape(bsz, G, nqb, SEL_QBLOCK, n_top).transpose(2, 0, 1, 3, 4)
    ok_b = sel_ok.reshape(bsz, G, nqb, SEL_QBLOCK, n_top).transpose(2, 0, 1, 3, 4)
    pos_b = pos.reshape(nqb, SEL_QBLOCK)
    gather = jax.vmap(jax.vmap(lambda blocks, ids: blocks[ids]))
    n_tok = n_top * SEL_BLOCK

    def sel_block(args):
        qb, ib, okb, pb = args
        kg = gather(k_blocks, ib)
        vg = gather(v_blocks, ib)
        s = jnp.einsum('bqghd,bgqkld->bghqkl', qb, kg).astype(jnp.float32) * scale
        tok = ib[..., None] * SEL_BLOCK + jnp.arange(SEL_BLOCK)
        m = okb[..., None] & (tok <= pb[None, None, :, None, None])
        p = masked_softmax(s.reshape(bsz, G, HG, SEL_QBLOCK, n_tok),
                           m.reshape(bsz, G, 1, SEL_QBLOCK, n_tok))
        return jnp.einsum('bghqn,bgqnd->bqghd', p, vg.reshape(bsz, G, SEL_QBLOCK, n_tok, DH))

    o_sel = lax.map(sel_block, (q_b, idx_b, ok_b, pos_b))
    o_sel = o_sel.transpose(1, 0, 2, 3, 4, 5).reshape(bsz, seq, G, HG, DH)

    k_win = apply_rope(rms_norm(kvh(kw_pre), knorm_g[2]), cos, sin)
    v_win = kvh(vw_pre)
    nwb = seq // WIN_QBLOCK
    span = WINDOW + WIN_QBLOCK
    kp = jnp.pad(k_win, ((0, 0), (WINDOW, 0), (0, 0), (0, 0)))
    vp = jnp.pad(v_win, ((0, 0), (WINDOW, 0), (0, 0), (0, 0)))
    kidx = jnp.arange(nwb)[:, None] * WIN_QBLOCK + jnp.arange(span)[None, :]
    kb = kp[:, kidx]
    vb = vp[:, kidx]
    qw = q_rot.reshape(bsz, nwb, WIN_QBLOCK, G, HG, DH)
    s_w = jnp.einsum('bnqghd,bnkgd->bghnqk', qw, kb).astype(jnp.float32) * scale
    qpos = pos.reshape(nwb, WIN_QBLOCK)[:, :, None]
    kpos = (kidx - WINDOW)[:, None, :]
    wmask = (kpos <= qpos) & (kpos > qpos - WINDOW) & (kpos >= 0)
    p_w = masked_softmax(s_w, wmask)
    o_win = jnp.einsum('bghnqk,bnkgd->bnqghd', p_w, vb).reshape(bsz, seq, G, HG, DH)

    g = jax.nn.sigmoid(gate_pre.astype(jnp.float32)).reshape(bsz, seq, G, HG, 3, 1)
    o = g[..., 0, :] * o_cmp + g[..., 1, :] * o_sel + g[..., 2, :] * o_win
    return o.reshape(bsz, seq, MIX_WIDTH).astype(q_pre.dtype)

def retention_mixer(q_pre, k_pre, v_pre, g_pre, cos, sin, onorm_g):
    bsz, seq, _ = q_pre.shape
    heads = lambda t: t.reshape(bsz, seq, N_HEADS, HEAD_DIM)
    q = apply_rope(heads(q_pre), cos, sin).astype(jnp.float32)
    k = apply_rope(heads(k_pre), cos, sin).astype(jnp.float32) * (HEAD_DIM ** -0.5)
    v = heads(v_pre).astype(jnp.float32)
    log_gamma = jnp.log1p(-jnp.exp2(-5.0 - jnp.arange(N_HEADS, dtype=jnp.float32)))
    t = jnp.arange(CHUNK, dtype=jnp.float32)
    causal = jnp.tril(jnp.ones((CHUNK, CHUNK), dtype=bool))
    dec_in = jnp.exp(jnp.where(causal, log_gamma[:, None, None] * (t[:, None] - t[None, :]), -jnp.inf))
    dec_q = jnp.exp(log_gamma[:, None] * (t + 1.0))[:, :, None]
    dec_k = jnp.exp(log_gamma[:, None] * (CHUNK - 1.0 - t))[:, :, None]
    dec_state = jnp.exp(log_gamma * CHUNK)[:, None, None]

    def step(r, xs):
        qc, kc, vc = xs
        a = jnp.einsum('bhtd,bhsd->bhts', qc, kc) * dec_in
        o = jnp.einsum('bhts,bhse->bhte', a, vc) + jnp.einsum('bhtd,bhde->bhte', qc, r) * dec_q
        r = dec_state * r + jnp.einsum('bhsd,bhse->bhde', kc * dec_k, vc)
        return r, o

    r0 = jnp.zeros((bsz, N_HEADS, HEAD_DIM, HEAD_DIM), jnp.float32)
    _, o = lax.scan(step, r0, (to_chunks(q), to_chunks(k), to_chunks(v)))
    o = rms_norm(from_chunks(o), onorm_g.reshape(N_HEADS, HEAD_DIM)) * jax.nn.silu(heads(g_pre).astype(jnp.float32))
    return o.reshape(bsz, seq, MIX_WIDTH).astype(q_pre.dtype)

def peer_ffn(x, wq, sub_keys, u_tab, v_tab):
    bsz, seq, d = x.shape
    xt = x.reshape(bsz * seq // PEER_TCHUNK, PEER_TCHUNK, d)

    def chunk(xc):
        q = (xc @ wq).reshape(PEER_TCHUNK, PEER_HEADS, 2, PEER_QDIM // 2)
        s = jnp.einsum('thpd,hpnd->thpn', q, sub_keys).astype(jnp.float32)
        v1, i1 = lax.top_k(s[:, :, 0], PEER_TOPK)
        v2, i2 = lax.top_k(s[:, :, 1], PEER_TOPK)
        cand = (v1[..., :, None] + v2[..., None, :]).reshape(PEER_TCHUNK, PEER_HEADS, PEER_TOPK * PEER_TOPK)
        vals, pos = lax.top_k(cand, PEER_TOPK)
        e = jnp.take_along_axis(i1, pos // PEER_TOPK, axis=-1) * PEER_NKEYS + \
            jnp.take_along_axis(i2, pos % PEER_TOPK, axis=-1)
        g = jax.nn.softmax(vals, axis=-1)
        act = jax.nn.gelu(jnp.einsum('td,thkd->thk', xc, u_tab[e]).astype(jnp.float32), approximate=False)
        return jnp.einsum('thk,thkd->td', (g * act).astype(xc.dtype), v_tab[e])

    return lax.map(chunk, xt).reshape(bsz, seq, d)

def setup_inputs(seed: int = 0) -> dict:
    key = jax.random.key(seed)
    ks = jax.random.split(key, 24)
    nrm = lambda k, shape, s: jax.random.normal(k, shape, jnp.float32) * s
    gain = lambda k, shape: 1.0 + 0.02 * jax.random.normal(k, shape, jnp.float32)
    mlstm_gate_b = jnp.concatenate([
        nrm(ks[6], (DEPTH, N_HEADS), 0.1),
        jnp.linspace(3.0, 6.0, N_HEADS, dtype=jnp.float32)[None, :] + nrm(ks[7], (DEPTH, N_HEADS), 0.1)], axis=-1)
    return {
        'x': jax.random.normal(ks[0], (BATCH, SEQ, D_MODEL), jnp.float32),
        'norm1_g': gain(ks[1], (DEPTH, D_MODEL)),
        'w_in': nrm(ks[2], (DEPTH, D_MODEL, N_IN), D_MODEL ** -0.5),
        'hgrn_lb': nrm(ks[3], (DEPTH, MIX_WIDTH), 1.0),
        'hgrn_onorm_g': gain(ks[4], (DEPTH, MIX_WIDTH)),
        'mlstm_conv_w': nrm(ks[5], (DEPTH, CONV_W, 2 * MIX_WIDTH), CONV_W ** -0.5),
        'mlstm_conv_b': nrm(ks[8], (DEPTH, 2 * MIX_WIDTH), 0.01),
        'mlstm_gate_b': mlstm_gate_b,
        'mlstm_onorm_g': gain(ks[9], (DEPTH, MIX_WIDTH)),
        'nsa_qnorm_g': gain(ks[10], (DEPTH, HEAD_DIM)),
        'nsa_knorm_g': gain(ks[11], (DEPTH, 3, HEAD_DIM)),
        'nsa_cmp_pe': nrm(ks[12], (DEPTH, 2, CMP_LEN, HEAD_DIM), 0.1),
        'nsa_cmp_w': nrm(ks[13], (DEPTH, 2, CMP_LEN * HEAD_DIM, HEAD_DIM), (CMP_LEN * HEAD_DIM) ** -0.5),
        'ret_onorm_g': gain(ks[14], (DEPTH, MIX_WIDTH)),
        'w_up': nrm(ks[15], (DEPTH, N_MIXERS, MIX_WIDTH, D_MODEL), MIX_WIDTH ** -0.5),
        'w_gate': nrm(ks[16], (DEPTH, N_MIXERS, D_MODEL, D_MODEL), D_MODEL ** -0.5),
        'w_out': nrm(ks[17], (DEPTH, D_MODEL, D_MODEL), 0.5 * D_MODEL ** -0.5),
        'norm2_g': gain(ks[18], (DEPTH, D_MODEL)),
        'peer_wq': nrm(ks[19], (DEPTH, D_MODEL, PEER_HEADS * PEER_QDIM), D_MODEL ** -0.5),
        'peer_keys': nrm(ks[20], (DEPTH, PEER_HEADS, 2, PEER_NKEYS, PEER_QDIM // 2), (PEER_QDIM // 2) ** -0.5),
        'peer_u': nrm(ks[21], (DEPTH, PEER_EXPERTS, D_MODEL), D_MODEL ** -0.5),
        'peer_v': nrm(ks[22], (DEPTH, PEER_EXPERTS, D_MODEL), 0.2),
    }

def reference(x, norm1_g, w_in, hgrn_lb, hgrn_onorm_g, mlstm_conv_w, mlstm_conv_b, mlstm_gate_b,
              mlstm_onorm_g, nsa_qnorm_g, nsa_knorm_g, nsa_cmp_pe, nsa_cmp_w, ret_onorm_g, w_up,
              w_gate, w_out, norm2_g, peer_wq, peer_keys, peer_u, peer_v):
    seq = x.shape[1]
    cos, sin = rope_tables(seq)
    lb_cum = jnp.cumsum(jax.nn.softmax(hgrn_lb.astype(jnp.float32), axis=0), axis=0)
    lb_all = lb_cum - lb_cum[0:1]
    for l in range(DEPTH):
        xn = rms_norm(x, norm1_g[l])
        (hq, hf, hi, hg, mq, mk, mv, mi, mf, mo, nq, nkc, nvc, nks, nvs, nkw, nvw, ng,
         rq, rk, rv, rg) = jnp.split(xn @ w_in[l], IN_OFFSETS, axis=-1)
        outs = (
            hgrn2_mixer(hq, hf, hi, hg, lb_all[l], hgrn_onorm_g[l]),
            mlstm_mixer(mq, mk, mv, mi, mf, mo, mlstm_conv_w[l], mlstm_conv_b[l], mlstm_gate_b[l], mlstm_onorm_g[l]),
            nsa_mixer(nq, nkc, nvc, nks, nvs, nkw, nvw, ng, cos, sin, nsa_qnorm_g[l], nsa_knorm_g[l],
                      nsa_cmp_pe[l], nsa_cmp_w[l]),
            retention_mixer(rq, rk, rv, rg, cos, sin, ret_onorm_g[l]),
        )
        merged = sum(jax.nn.sigmoid(xn @ w_gate[l, m]) * (outs[m] @ w_up[l, m]) for m in range(N_MIXERS))
        x = x + merged @ w_out[l]
        x = x + peer_ffn(rms_norm(x, norm2_g[l]), peer_wq[l], peer_keys[l], peer_u[l], peer_v[l])
    return x


_drawn_inputs = setup_inputs


def setup_inputs(seed=0):
    import zlib

    import numpy as np

    out = dict(_drawn_inputs(seed))
    spreads = {}
    factors = {'norm1_g': 3.773,
     'hgrn_onorm_g': 32.523,
     'mlstm_conv_b': 64.0,
     'mlstm_onorm_g': 64.0,
     'nsa_qnorm_g': 25.091,
     'nsa_knorm_g': 25.832,
     'nsa_cmp_pe': 26.393,
     'ret_onorm_g': 32.519,
     'norm2_g': 33.328}
    for name, (base, spread) in spreads.items():
        noise = np.random.default_rng([zlib.crc32(name.encode()), seed]).standard_normal(out[name].shape)
        drawn = base * np.exp(spread * noise) if base else spread * noise
        out[name] = __import__('jax').numpy.asarray(drawn.astype(out[name].dtype))
    for name, factor in factors.items():
        out[name] = (out[name] * factor).astype(out[name].dtype)
    return out
```

```python
from contextlib import ExitStack

import concourse.bass as bass
from concourse import mybir

F32 = mybir.dt.float32
BF16 = mybir.dt.bfloat16
U32 = mybir.dt.uint32
ALU = mybir.AluOpType
ACT = mybir.ActivationFunctionType
AX = mybir.AxisListType.X

P = 128
T = 256
NT = T // P
D = 1024
KD = D // P
H = 4
HD = 64
NCMP = 15
CMPL = 32
CMPS = 16
PH = 8
PK = 16
NK = 128
EPS = 1e-6
NEG = -1e30
GONE = -3e38
SCALE = HD ** -0.5
SLOT = 4096
WSLOTS = 3
GROUP = 2
NG = NK // GROUP
URING = 4
TB = 8
NJ = NK // 2
NS = T // TB

WIDTHS = dict(hq=256, hf=256, hi=256, hg=256, mq=256, mk=256, mv=256, mi=4, mf=4, mo=256, nq=256,
              kc=128, vc=128, ks=128, vs=128, kw=128, vw=128, ng=12, rq=256, rk=256, rv=256, rg=256)
PROJ = [("hf", "hq"), ("rq", "rk"), ("nq", "ks", "kw"), ("mq", "mk"), ("kc", "vc", "mi", "mf", "ng"),
        ("rv", "hi"), ("vs", "vw", "mv"), ("hg", "mo"), ("rg",)]
RET, HG, ML, NSA = 3, 0, 1, 2
ORDER = [RET, HG, ML, NSA]

CONST_LATE = dict(ident=128, iota=128, iota16=16)
CONST_FRONT = dict(cos=64, sin=64, mneg=128, c01=384, retd=1536, reset=256, ones=256, cmpneg=32,
                   cmp01=32, sel=512, level=1024)
PARAMS = dict(g1=8, cw=16, cb=4, pe=64, gb=2, gh=256, gm=256, gr=256, gqk=512, gkc=128)

N_PROJ = 18
N_GATE = 16
SLOT_LAST = [1, 3, 5, 7, 10, 12, 14, 16, 17]
LEVELS = [0, 1, 2, 4, 8, 16, 32, 64, 128]
TR = {n: i for i, n in enumerate(
    ["rq", "rk", "qrot", "q", "ks", "kw", "mlgate", "mlden", "kcmp", "pc0", "pc1",
     "s0", "s1a", "s1b", "o3", "o0", "o1", "w0", "w1a", "w1b", "o2", "i", "g"])}
AV = {n: i for i, n in enumerate(["hg", "ret", "ml", "cmp", "sel", "win"])}


def offsets(table):
    out, at = {}, 0
    for name, n in table.items():
        out[name] = (at, n)
        at += n
    return out, at


def bcast(ap, n):
    return ap.unsqueeze(ap.ndim).to_broadcast([*ap.shape, n])


def repeat(ap, n, axis=1):
    shape = [*ap.shape]
    shape.insert(axis, n)
    return ap.unsqueeze(axis).to_broadcast(shape)


def build(nc, x, w_in, w_cmp, w_gate, w_up, w_out, wq, keys, u_tab, v_tab, g2, late, front, params, out):
    off_late, n_late = offsets(CONST_LATE)
    off_front, n_front = offsets(CONST_FRONT)
    off_par, n_par = offsets(PARAMS)
    with ExitStack() as ctx:
        def sem(name):
            return ctx.enter_context(nc.semaphore(name))

        TOP = 53200
        arena = ctx.enter_context(nc.sbuf_tensor("arena", [P, TOP], F32))
        ps = ctx.enter_context(nc.psum_tensor("ps", [P, 8, 512], F32))

        class Region:
            def __init__(self, start, end):
                self.at, self.end = start, end

            def take(self, n):
                a = self.at
                self.at += n
                assert self.at <= self.end, (self.at, self.end)
                return arena[:, a:a + n]

        hbuf = arena[:, 0:NK * T].rearrange("p (j t) -> p j t", t=T)
        peer = Region(NK * T, TOP)
        uring = peer.take(URING * GROUP * D).rearrange("p (s j n) -> p s j n", s=URING, j=GROUP)
        whi = peer.take(GROUP * D).bitcast(BF16).rearrange("p (s j n) -> p s j n", s=2, j=GROUP)
        wlo = peer.take(GROUP * D).bitcast(BF16).rearrange("p (s j n) -> p s j n", s=2, j=GROUP)
        xhi = peer.take(D).bitcast(BF16).rearrange("p (k t) -> p k t", k=KD)
        xlo = peer.take(D).bitcast(BF16).rearrange("p (k t) -> p k t", k=KD)
        ahi = xhi.rearrange("p k t -> p (k t)")[:, 0:2 * GROUP * T].rearrange("p (s j t) -> p s j t", s=2, j=GROUP)
        alo = xlo.rearrange("p k t -> p (k t)")[:, 0:2 * GROUP * T].rearrange("p (s j t) -> p s j t", s=2, j=GROUP)
        i1T, i2T, ghT, glT = (peer.take(T) for _ in range(4))
        iota_bf = peer.take(64).bitcast(BF16)
        oh1h, oh1l, oh2 = (peer.take(TB * n).bitcast(BF16).rearrange("p (s t n) -> p s t n", s=2, t=TB)
                           for n in (NK, NK, NJ))
        top = peer.at
        xres = peer.take(NT * D).rearrange("p (a n) -> p a n", a=NT)
        late_sb = peer.take(n_late)
        g2_sb = peer.take(KD)
        rt = Region(16384, 32768)
        qT = arena[:, 12288:16384].rearrange("p (c t) -> p c t", t=T)
        xn2T = rt.take(KD * T).rearrange("p (k t) -> p k t", k=KD)
        rt_big = rt.take(2048)
        s_sb = rt.take(NT * 16 * NK).rearrange("p (a c n) -> p a c n", a=NT, c=16)
        rep = rt.take(2 * 256).rearrange("p (s n) -> p s n", s=2)
        cand = rt.take(256)
        v16 = rt.take(NT * 16 * PK).rearrange("p (a c k) -> p a c k", a=NT, c=16)
        iu = rt.take(NT * 16 * PK).bitcast(U32).rearrange("p (a c k) -> p a c k", a=NT, c=16)
        if_ = rt.take(NT * 16 * PK).rearrange("p (a c k) -> p a c k", a=NT, c=16)
        vals = rt.take(NT * PH * PK).rearrange("p (a c k) -> p a c k", a=NT, c=PH)
        pos = rt.take(NT * PH * PK).bitcast(U32).rearrange("p (a c k) -> p a c k", a=NT, c=PH)
        posr = rt.take(256).bitcast(U32)
        posf = rt.take(256)
        picked = rt.take(2 * 256).rearrange("p (w a n) -> p w a n", w=2, a=NT)
        zs = rt.take(32)
        fr = Region(0, top)
        wring = fr.take(WSLOTS * SLOT).rearrange("p (s n) -> p s n", s=WSLOTS)
        gates_w = fr.take(4 * KD * T)
        gates = gates_w.rearrange("p (m k t) -> p m k t", m=4, k=KD)
        xnT = fr.take(KD * T).rearrange("p (k t) -> p k t", k=KD)
        outsT = fr.take(4 * 2 * T).rearrange("p (m f t) -> p m f t", m=4, f=2)
        front_sb = fr.take(n_front)
        par_sb = fr.take(n_par)
        fm_h = fr.take(1024).rearrange("p (w n) -> p w n", w=2)
        fm_m = fr.take(1024).rearrange("p (f t) -> p f t", f=4)
        fm_c = fr.take(512).rearrange("p (w t) -> p w t", w=2)
        tm = fr.take(NT * 1024).rearrange("p (a n) -> p a n", a=NT)
        tmv = fr.take(NT * 1024).rearrange("p (a n) -> p a n", a=NT)
        tmg = fr.take(NT * 780).rearrange("p (a n) -> p a n", a=NT)
        attT = fr.take(6 * 512).rearrange("p (w f t) -> p w f t", w=6, f=2)
        bufA, bufB, bufC, bufD = (fr.take(n) for n in (1536, 1536, 1024, 1024))
        kcp = fm_h.rearrange("p w (a t) -> p w a t", a=2)
        mtmp = bufA.rearrange("p (s n) -> p s n", s=3)
        obuf = fr.take(4 * 512).rearrange("p (m n) -> p m n", m=4)
        sqb = fr.take(512)
        small = fr.take(512)

        def const(name):
            o, n = (off_late if name in off_late else off_front)[name]
            return (late_sb if name in off_late else front_sb)[:, o:o + n]

        def par(name):
            o, n = off_par[name]
            return par_sb[:, o:o + n]

        ident = const("ident")
        xs1 = arena[:, 8192:10240].rearrange("p (a n) -> p a n", a=NT)
        xs2 = rt_big.rearrange("p (a n) -> p a n", a=NT)
        hgr = gates_w
        hg_bc = hgr[:, 0:512]
        hg_q, hg_k = hgr[:, 512:1024], hgr[:, 1024:1536]
        hg_d = hgr[:, 1536:2560].rearrange("p (s n) -> p s n", s=2)
        hg_e = hgr[:, 2560:3584].rearrange("p (s n) -> p s n", s=2)
        hg_qe = hgr[:, 3584:4608].rearrange("p (s n) -> p s n", s=2)
        hg_ke = hgr[:, 4608:5632].rearrange("p (s n) -> p s n", s=2)
        hg_a = hgr[:, 5632:6656]
        hg_off = hgr[:, 6656:7168]
        hg_t = hgr[:, 7168:7680]
        hg_tot = small[:, 16:18]
        rows = hgr[:, 768:2560].rearrange("p (w t) -> p w t", w=7)
        sgb = tm.rearrange("p a n -> p (a n)")[:, 0:NT * 780].rearrange("p (a n) -> p a n", a=NT)
        ropes = [b[:, 0:1024].rearrange("p (a h n) -> p a h n", a=NT, h=16) for b in (bufA, bufB, bufC)]
        ropes.append(bufD[:, 0:1024].rearrange("p (a h n) -> p a h n", a=NT, h=16))
        r16 = small[:, 408:424]
        r8 = small[:, 440:448]
        kdup = obuf[:, 0:2, :].rearrange("p m n -> p (m n)").rearrange("p (a h r n) -> p a h r n", a=NT, h=4, r=2)
        qn = obuf[:, 2, :].rearrange("p (a n) -> p a n", a=NT)
        tmh = tm.rearrange("p a (h n) -> p a h n", n=HD)
        cv = bufC[:, 0:1024].rearrange("p (f t) -> p f t", f=4)
        csg = bufD[:, 0:1024].rearrange("p (f t) -> p f t", f=4)
        retA = bufA.rearrange("p (h n) -> p h n", h=H)
        mlW = bufB.rearrange("p (h n) -> p h n", h=H)
        gcol = small[:, 32:40]
        enm = small[:, 40:48]
        att_s = [bufA[:, 0:1024], bufB[:, 0:1024]]
        att_p = [bufC[:, 0:1024], bufD[:, 0:1024]]
        zsum = small[:, 64:88].rearrange("p (i n) -> p i n", i=3)
        nmx = small[:, 96:112].rearrange("p (i n) -> p i n", i=2)
        kcs = small[0:NCMP, 128:384].rearrange("p (w n) -> p w n", w=2)
        cmpS = sqb[:, 0:128]
        cmpT = sqb[:, 128:256]
        kcn = bufA[0:NCMP, 1024:1280]
        kcT = bufA[:, 1280:1312]
        pcT = bufB[0:NCMP, 0:1024]
        wslot = lambda n: wring[:, n % WSLOTS, :]

        def head_norm(o):
            return o.rearrange("p (g n) -> p g n", n=HD)

        def scored(ap4):
            return ps[:, 2:6, 0:384]

        x_loaded, consts_loaded, stored = sem("x_loaded"), sem("consts_loaded"), sem("stored")
        w_loaded = [sem(f"w_loaded{i}") for i in range(WSLOTS)]
        u_loaded = [sem(f"u_loaded{i}") for i in range(URING)]
        dve_done, act_done, pool_done = sem("dve_done"), sem("act_done"), sem("pool_done")
        rms_ready, root_ready, xs_ready = sem("rms_ready"), sem("root_ready"), sem("xs_ready")
        xt_full, xn_ready = sem("xt_full"), sem("xn_ready")
        proj_full, proj_done = sem("proj_full"), sem("proj_done")
        hg_logs, hg_sigs, hg_q_ready = sem("hg_logs"), sem("hg_sigs"), sem("hg_q_ready")
        hg_d_ready, hg_e_ready = sem("hg_d_ready"), sem("hg_e_ready")
        hg_qe_ready, hg_ke_ready = sem("hg_qe_ready"), sem("hg_ke_ready")
        hg_full, hg_copied = sem("hg_full"), sem("hg_copied")
        qk_ms_ready, qk_root = sem("qk_ms_ready"), sem("qk_root")
        qk_normed, rope_pool, roped, kdup_ready, qn_ready = (sem("qk_normed"), sem("rope_pool"), sem("roped"),
                                                             sem("kdup_ready"), sem("qn_ready"))
        tr_full, tr_taken = sem("tr_full"), sem("tr_taken")
        av_full, av_taken = sem("av_full"), sem("av_taken")
        o_square, o_ms, o_root, o_ready = sem("o_square"), sem("o_ms"), sem("o_root"), sem("o_ready")
        ret_full, ret_a_ready = sem("ret_full"), sem("ret_a_ready")
        conv_done, conv_sig, conv_ready = sem("conv_done"), sem("conv_sig"), sem("conv_ready")
        ml_f, ml_logs, ml_rows = sem("ml_f"), sem("ml_logs"), sem("ml_rows")
        ml_bc_full, ml_d_ready, ml_e_ready, ml_full, ml_w_ready = (
            sem("ml_bc_full"), sem("ml_d_ready"), sem("ml_e_ready"), sem("ml_full"), sem("ml_w_ready"))
        sig_ready, gate_ready = sem("sig_ready"), sem("gate_ready")
        kcp_ready, cmp_full, cmp_out, kc_ms, kc_root, kc_ready = (
            sem("kcp_ready"), sem("cmp_full"), sem("cmp_out"), sem("kc_ms"), sem("kc_root"), sem("kc_ready"))
        cs_full, cs_ready, ce_ready, pc_ready = sem("cs_full"), sem("cs_ready"), sem("ce_ready"), sem("pc_ready")
        att_full, att_max, att_exp = sem("att_full"), sem("att_max"), sem("att_exp")
        up_full, up_mul, up_add = sem("up_full"), sem("up_mul"), sem("up_add")
        y_full, y_taken = sem("y_full"), sem("y_taken")
        xhi_ready, xlo_ready = sem("xhi_ready"), sem("xlo_ready")
        q_full, q_done, s_full, s_done = sem("q_full"), sem("q_done"), sem("s_full"), sem("s_done")
        vals_ready, g_exp, routed = sem("vals_ready"), sem("g_exp"), sem("routed")
        hi_ready, lo_ready = sem("hi_ready"), sem("lo_ready")
        ahi_ready, alo_ready = sem("ahi_ready"), sem("alo_ready")
        group_full, gelu_done = sem("group_full"), sem("gelu_done")
        oh_ready, g_full, g_taken, y2_full, y2_ready = (sem("oh_ready"), sem("g_full"), sem("g_taken"),
                                                        sem("y2_full"), sem("y2_ready"))

        stream = [(w_in[i], SLOT, (proj_full, SLOT_LAST[i] + 1)) for i in range(len(PROJ))]
        stream += [(w_cmp, SLOT, (cmp_full, 1))]
        CMP_SLOT = len(stream) - 1
        GATE_SLOT = len(stream)
        stream += [(w_gate[i], SLOT, (proj_full, N_PROJ + 2 * (i + 1))) for i in range(8)]
        UP_SLOT = len(stream)
        stream += [(w_up[i], SLOT, (up_full, 8 * (i + 1))) for i in range(2)]
        OUT_SLOT = len(stream)
        stream += [(w_out[i], SLOT, (y_full, 2 * (i + 1))) for i in range(2)]
        WQ_SLOT = len(stream)
        stream += [(wq[i], SLOT, (q_full, 2 * (i + 1))) for i in range(4)]
        KEY_SLOT = len(stream)
        stream += [(keys, 16 * NK, None)]

        def wait_slot(eng, n):
            eng.wait_ge(w_loaded[n % WSLOTS], 16 * (n // WSLOTS + 1))

        block = ctx.enter_context(nc.Block())

        @block.sync
        def _(sp):
            sp.dma_start(xres, x).then_inc(x_loaded, 16)
            for dst, src in ((late_sb, late), (front_sb, front), (par_sb, params), (g2_sb, g2)):
                sp.dma_start(dst, src).then_inc(consts_loaded, 16)
            for n, (src, size, _free) in enumerate(stream):
                if n >= WSLOTS:
                    free, value = stream[n - WSLOTS][2]
                    sp.wait_ge(free, value)
                elif n == 2:
                    sp.wait_ge(xt_full, 1)
                sp.dma_start(wslot(n)[:, 0:size], src).then_inc(w_loaded[n % WSLOTS], 16)
                if n == WQ_SLOT:
                    sp.wait_ge(up_add, 12)
                    sp.wait_ge(up_mul, 16)
                    for s in range(URING):
                        sp.dma_start(uring[:, s], u_tab[s].rearrange("p (j n) -> p j n", j=GROUP)
                                     ).then_inc(u_loaded[s], 16)

            for a in range(NT):
                sp.wait_ge(y2_ready, a + 1)
                sp.dma_start(out[a * P:(a + 1) * P, :], xres[:, a, :]).then_inc(stored, 16)
            sp.wait_ge(stored, 16 * NT)

        @block.tensor
        def _(pe):
            mm, tp = nc.tensor.matmul, nc.tensor.transpose

            def turn_x(src, ready_at):
                pe.wait_ge(xs_ready, ready_at)
                for k in range(KD):
                    for a in range(NT):
                        last = tp(ps[:, 2 + k // 2, (k % 2) * T + a * P:(k % 2) * T + (a + 1) * P],
                                  src[:, a, k * P:(k + 1) * P], ident)
                last.then_inc(xt_full, 1)

            def feature_tiles(bank, w, cols, rhs=xnT, width=P):
                for i, c in enumerate(cols):
                    for k in range(KD):
                        last = mm(ps[0:width, bank, i * T:(i + 1) * T], w[:, k, c:c + width], rhs[:, k, :],
                                  start=(k == 0), stop=(k == KD - 1))
                return last

            def token_tile(bank, col, w, a, c0, n, src=xnT):
                for k in range(KD):
                    last = mm(ps[:, bank, col:col + n], src[:, k, a * P:(a + 1) * P], w[:, k, c0:c0 + n],
                              start=(k == 0), stop=(k == KD - 1))
                return last

            def proj(u):
                slot = [s for s, e in enumerate(SLOT_LAST) if u <= e][0]
                wait_slot(pe, slot)
                if u >= 2:
                    pe.wait_ge(proj_done, u - 1)
                b = u % 2
                w = wslot(slot).rearrange("p (k n) -> p k n", k=KD)
                if u in (0, 1, 6, 7, 8):
                    c = {0: 0, 1: 256, 6: 0, 7: 256, 8: 0}[u]
                    last = feature_tiles(b, w, (c, c + P))
                elif u == 9:
                    last = feature_tiles(b, w, (256, 260), width=4)
                elif u == 10:
                    for a in range(NT):
                        last = token_tile(b, 12 * a, w, a, 264, 12)
                elif u == 17:
                    for a in range(NT):
                        last = token_tile(b, 256 * a, w, a, 0, 256)
                else:
                    a = {2: 0, 3: 1, 4: 0, 5: 1, 11: 0, 12: 1, 13: 0, 14: 1, 15: 0, 16: 1}[u]
                    last = token_tile(b, 0, w, a, 0, 512)
                last.then_inc(proj_full, 1)

            def gate(i):
                u = N_PROJ + i
                wait_slot(pe, GATE_SLOT + i // 2)
                pe.wait_ge(proj_done, u - 1)
                w = wslot(GATE_SLOT + i // 2).rearrange("p (k n) -> p k n", k=KD)
                c = (i % 2) * 256
                feature_tiles(u % 2, w, (c, c + P)).then_inc(proj_full, 1)

            def hg_level(li):
                if li == 0:
                    pe.wait_ge(hg_sigs, 1)
                    pe.wait_ge(hg_q_ready, 1)
                    q, k = hg_q, hg_k
                else:
                    pe.wait_ge(hg_qe_ready, li)
                    pe.wait_ge(hg_ke_ready, li)
                    q, k = hg_qe[:, li % 2, :], hg_ke[:, li % 2, :]
                if li >= 2:
                    pe.wait_ge(hg_copied, li - 1)
                b = 2 + 2 * (li % 2)
                for f in range(2):
                    for par_ in range(2):
                        r = slice(64 * par_, 64 * par_ + 64)
                        if LEVELS[li] == 128:
                            last = mm(ps[:, b + par_, f * P:(f + 1) * P], k[r, f * T:f * T + P],
                                      q[r, f * T + P:f * T + T], start=True, stop=True)
                            continue
                        for st in range(2):
                            c = f * T + st * P
                            last = mm(ps[:, b + par_, c:c + P], k[r, c:c + P], q[r, c:c + P],
                                      start=True, stop=True)
                last.then_inc(hg_full, 1)

            def av(name, weights, values, blocks=None):
                n = AV[name]
                if n >= 1:
                    pe.wait_ge(av_taken, n)
                for a in range(NT):
                    for h in range(H):
                        parts = range(a + 1)
                        for s in parts:
                            last = mm(ps[:, 7, a * 256 + h * HD:a * 256 + (h + 1) * HD], weights(a, s, h),
                                      values(s, h), start=(s == 0), stop=(s == a))
                last.then_inc(av_full, 1)

            def tri(buf):
                return lambda a, s, h: buf[:, h, (a + s) * P:(a + s + 1) * P]

            def tr_begin(name):
                if TR[name]:
                    pe.wait_ge(tr_taken, TR[name])

            def turn_heads(name, src):
                tr_begin(name)
                for f in range(2):
                    for a in range(NT):
                        last = tp(ps[:, 6, f * T + a * P:f * T + (a + 1) * P], src(f, a), ident)
                last.then_inc(tr_full, 1)

            def full_scores(q, k, full):
                for h in range(H):
                    f, r = h // 2, slice(64 * (h % 2), 64 * (h % 2) + 64)
                    mm(ps[:, 2 + h, 0:T], k[r, f, 0:P], q[r, f, :], start=True, stop=True)
                    last = mm(ps[:, 2 + h, T:T + P], k[r, f, P:T], q[r, f, P:T], start=True, stop=True)
                last.then_inc(full, 1)

            def att_scores(n, which, a):
                b = 2 + 2 * (n % 2)
                if n >= 2:
                    pe.wait_ge(att_max, n - 1)
                for h in range(H):
                    f, r = h // 2, slice(64 * (h % 2), 64 * (h % 2) + 64)
                    w = (a + 1) * P
                    last = mm(ps[:, b + h % 2, f * T:f * T + w], attT[r, 2, f, a * P:(a + 1) * P],
                              attT[r, 4 + which, f, 0:w], start=True, stop=True)
                last.then_inc(att_full, 1)

            def att_turn(n, a, names):
                pe.wait_ge(att_exp, n + 1)
                p = att_s[n % 2].rearrange("p (h n) -> p h n", h=H)
                for s, name in enumerate(names):
                    tr_begin(name)
                    for h in range(H):
                        last = tp(ps[:, 6, h * P:(h + 1) * P], p[:, h, s * P:(s + 1) * P], ident)
                    last.then_inc(tr_full, 1)

            def att_av(name, n, a, taken):
                pe.wait_ge(tr_taken, taken)
                if a == 0:
                    pe.wait_ge(av_taken, AV[name])
                p = att_p[n % 2].rearrange("p (s h n) -> p s h n", s=2, h=H)
                c0 = 512 if name == "sel" else 640
                for h in range(H):
                    g = c0 - 0 + (h // 2) * HD
                    for s in range(a + 1):
                        last = mm(ps[:, 7, a * 256 + h * HD:a * 256 + (h + 1) * HD], p[:, s, h, :],
                                  tmv[:, s, g:g + HD], start=(s == 0), stop=(s == a))
                if a == 1:
                    last.then_inc(av_full, 1)

            def turn_out(name, m, ready_at):
                pe.wait_ge(o_ready, ready_at)
                turn_heads(name, lambda f, a: obuf[:, m, a * 256 + f * P:a * 256 + (f + 1) * P])

            pe.wait_ge(consts_loaded, 64)
            turn_x(xs1, 2)
            pe.wait_ge(xn_ready, 2)
            proj(0), proj(1), proj(2), proj(3)
            hg_level(0), hg_level(1)
            proj(4), proj(5)
            hg_level(2), hg_level(3), hg_level(4)
            proj(6), proj(7)
            hg_level(5), hg_level(6), hg_level(7), hg_level(8)
            proj(8), proj(9), proj(10), proj(11), proj(12)
            pe.wait_ge(hg_copied, 9)
            pe.wait_ge(proj_done, 13)
            hg_a4 = hg_a.rearrange("p (r f s n) -> p r f s n", r=2, f=2, s=2)
            hg_off3 = hg_off.rearrange("p (r f n) -> p r f n", r=2, f=2)
            av("hg", lambda a, s, h: hg_off3[:, h % 2, h // 2, :] if a != s else hg_a4[:, h % 2, h // 2, a, :],
               lambda s, h: tmv[:, s, 256 + h * HD:256 + (h + 1) * HD])
            pe.wait_ge(roped, 2)
            for name, c in (("rq", 0), ("rk", 256), ("qrot", 512)):
                turn_heads(name, lambda f, a, c=c: tm[:, a, c + f * P:c + (f + 1) * P])
            pe.wait_ge(qn_ready, 1)
            turn_heads("q", lambda f, a: qn[:, a, f * P:(f + 1) * P])
            pe.wait_ge(kdup_ready, 2)
            for w, name in enumerate(("ks", "kw")):
                turn_heads(name, lambda f, a, w=w: kdup[:, a, 2 * w + f].rearrange("p r n -> p (r n)"))
            pe.wait_ge(tr_taken, TR["rk"] + 1)
            full_scores(attT[:, 0], attT[:, 1], ret_full)
            proj(13), proj(14)
            pe.wait_ge(ret_a_ready, 1)
            av("ret", tri(retA), lambda s, h: tmv[:, s, h * HD:(h + 1) * HD])
            pe.wait_ge(ml_rows, 1)
            tr_begin("mlgate")
            for i, r in enumerate((5, 0)):
                for a in range(NT):
                    last = tp(ps[:, 6, 8 * i + 4 * a:8 * i + 4 * a + 4], rows[0:4, r, a * P:(a + 1) * P],
                              ident[0:4, 0:4])
            last.then_inc(tr_full, 1)
            for h in range(H):
                last = mm(ps[:, 2 + h // 2, (h % 2) * T:(h % 2 + 1) * T], const("sel")[0:4, h * P:(h + 1) * P],
                          rows[0:4, 2, :], start=True, stop=True)
            last.then_inc(ml_bc_full, 1)
            proj(15), proj(16), proj(17)
            pe.wait_ge(conv_ready, 1)
            pe.wait_ge(ml_d_ready, 1)
            full_scores(cv[:, 0:2], cv[:, 2:4], ml_full)
            wait_slot(pe, CMP_SLOT)
            pe.wait_ge(kcp_ready, 4)
            pe.wait_ge(ml_w_ready, 1)
            wc = wslot(CMP_SLOT).rearrange("p (w l n) -> p w l n", w=2, l=CMPL)
            for w in range(2):
                for l in range(CMPL):
                    for g in range(2):
                        r = slice(64 * g, 64 * g + 64)
                        last = mm(ps[0:NCMP, 2 + g, w * HD:(w + 1) * HD],
                                  kcp[r, w, l // CMPS, l % CMPS + (l // CMPS) * CMPS:
                                      l % CMPS + (l // CMPS) * CMPS + CMPS * (NCMP - 1) + 1:CMPS],
                                  wc[r, w, l, :], start=(l == 0), stop=(l == CMPL - 1))
            last.then_inc(cmp_full, 1)
            tr_begin("mlden")
            ones = const("ones")
            for a in range(NT):
                for h in range(H):
                    for s in range(a + 1):
                        last = mm(ps[:, 6, 4 * a + h:4 * a + h + 1], tri(mlW)(a, s, h), ones[:, 0:1],
                                  start=(s == 0), stop=(s == a))
            last.then_inc(tr_full, 1)
            av("ml", tri(mlW), lambda s, h: tmv[:, s, 768 + h * HD:768 + (h + 1) * HD])
            gate(0), gate(1)
            pe.wait_ge(kc_ready, 1)
            tr_begin("kcmp")
            for g in range(2):
                last = tp(ps[:, 6, g * 16:g * 16 + NCMP],
                          kcn.rearrange("p (g n) -> p g n", g=2)[:, g, :], ident[0:NCMP, 0:NCMP])
            last.then_inc(tr_full, 1)
            gate(2)
            pe.wait_ge(tr_taken, TR["kcmp"] + 1)
            for a in range(NT):
                for h in range(H):
                    f, r = h // 2, slice(64 * (h % 2), 64 * (h % 2) + 64)
                    last = mm(ps[:, 4 + h % 2, a * 32 + f * 16:a * 32 + f * 16 + NCMP],
                              attT[r, 3, f, a * P:(a + 1) * P], kcT[r, f * 16:f * 16 + NCMP],
                              start=True, stop=True)
            last.then_inc(cs_full, 1)
            gate(3)
            pe.wait_ge(pc_ready, 1)
            for a in range(NT):
                tr_begin(f"pc{a}")
                for h in range(H):
                    c = (a * H + h) * 16
                    last = tp(ps[0:NCMP, 6, h * P:(h + 1) * P], cmpT[:, c:c + NCMP], ident)
                last.then_inc(tr_full, 1)
            pe.wait_ge(cs_ready, 1)
            att_scores(0, 0, 0)
            gate(4)
            pe.wait_ge(tr_taken, TR["pc1"] + 1)
            pe.wait_ge(av_taken, AV["cmp"])
            for a in range(NT):
                for h in range(H):
                    last = mm(ps[:, 7, a * 256 + h * HD:a * 256 + (h + 1) * HD],
                              pcT[:, (a * H + h) * P:(a * H + h + 1) * P],
                              kcs[:, 1, (h // 2) * HD:(h // 2 + 1) * HD], start=True, stop=True)
            last.then_inc(av_full, 1)
            att_scores(1, 0, 1)
            gate(5)
            att_turn(0, 0, ["s0"])
            gate(6)
            att_turn(1, 1, ["s1a", "s1b"])
            att_av("sel", 0, 0, TR["s0"] + 1)
            att_scores(2, 1, 0)
            gate(7)
            att_av("sel", 1, 1, TR["s1b"] + 1)
            gate(8)
            turn_out("o3", RET, 1)
            turn_out("o0", HG, 2)
            gate(9)
            att_scores(3, 1, 1)
            gate(10)
            turn_out("o1", ML, 3)
            gate(11)
            att_turn(2, 0, ["w0"])
            gate(12)
            att_turn(3, 1, ["w1a", "w1b"])
            att_av("win", 2, 0, TR["w0"] + 1)
            gate(13)
            att_av("win", 3, 1, TR["w1b"] + 1)
            gate(14), gate(15)

            def ups(i):
                m = ORDER[i]
                wait_slot(pe, UP_SLOT + i // 2)
                w = wslot(UP_SLOT + i // 2).rearrange("p (m k n) -> p m k n", m=2, k=2)
                for c in range(4):
                    u = 4 * i + c
                    if u >= 2:
                        pe.wait_ge(up_mul, u - 1)
                    for n in range(2):
                        for k in range(2):
                            col = (2 * c + n) * P
                            last = mm(ps[:, u % 2, n * T:(n + 1) * T], w[:, i % 2, k, col:col + P],
                                      outsT[:, m, k, :], start=(k == 0), stop=(k == 1))
                    last.then_inc(up_full, 1)

            pe.wait_ge(proj_done, N_PROJ + N_GATE)
            pe.wait_ge(tr_taken, TR["o1"] + 1)
            ups(0), ups(1), ups(2)
            turn_out("o2", NSA, 4)
            pe.wait_ge(tr_taken, TR["o2"] + 1)
            ups(3)
            pe.wait_ge(up_mul, 16)
            pe.wait_ge(up_add, 12)
            for i in range(2):
                wait_slot(pe, OUT_SLOT + i)
                w = wslot(OUT_SLOT + i).rearrange("p (k n) -> p k n", k=KD)
                for a in range(NT):
                    u = 2 * i + a
                    if u >= 2:
                        pe.wait_ge(y_taken, u - 1)
                    token_tile(u % 2, 0, w, a, 0, 512).then_inc(y_full, 1)
            turn_x(xs2, 4)
            pe.wait_ge(xn_ready, 4)
            pe.wait_ge(y_taken, 4)
            for u in range(8):
                wait_slot(pe, WQ_SLOT + u // 2)
                if u >= 2:
                    pe.wait_ge(q_done, u - 1)
                w = wslot(WQ_SLOT + u // 2).rearrange("p (k n) -> p k n", k=KD)
                c = (u % 2) * 256
                feature_tiles(u % 2, w, (c, c + P), rhs=xn2T).then_inc(q_full, 1)
            wait_slot(pe, KEY_SLOT)
            pe.wait_ge(q_done, 8)
            kk = wslot(KEY_SLOT)[:, 0:16 * NK].rearrange("p (c n) -> p c n", c=16)
            for u in range(8):
                a, c4 = u // 4, u % 4
                if u >= 4:
                    pe.wait_ge(s_done, u - 3)
                for c in range(4):
                    last = mm(ps[:, 2 + c4, c * NK:(c + 1) * NK], qT[:, 4 * c4 + c, a * P:(a + 1) * P],
                              kk[:, 4 * c4 + c, :], start=True, stop=True)
                last.then_inc(s_full, 1)
            pe.wait_ge(xhi_ready, 1)
            pe.wait_ge(xlo_ready, 1)

            def u_group(s, g, gelus=True):
                if gelus:
                    pe.wait_ge(gelu_done, g - 1)
                for j in range(GROUP):
                    pe.wait_ge(lo_ready, g * GROUP + j + 1)
                    for k in range(KD):
                        o = ps[:, s % 2, j * T:(j + 1) * T]
                        h_, l_ = whi[:, s % 2, j, k * P:(k + 1) * P], wlo[:, s % 2, j, k * P:(k + 1) * P]
                        mm(o, h_, xhi[:, k, :], start=(k == 0), stop=False)
                        mm(o, h_, xlo[:, k, :], start=False, stop=False)
                        last = mm(o, l_, xhi[:, k, :], start=False, stop=(k == KD - 1))
                last.then_inc(group_full, 1)

            def spread(s, n):
                pe.wait_ge(oh_ready, n + 1)
                for t in range(TB):
                    o = ps[:, 6 + s % 2, t * NJ:(t + 1) * NJ]
                    mm(o, oh1h[:, s % 2, t, :], oh2[:, s % 2, t, :], start=True, stop=False)
                    last = mm(o, oh1l[:, s % 2, t, :], oh2[:, s % 2, t, :], start=False, stop=True)
                last.then_inc(g_full, 1)

            for s in range(4):
                u_group(s, s, gelus=s >= 2)
            with pe.Fori(1, NG // 8) as i:
                for s in range(4):
                    u_group(s, i * 4 + s)
            pe.wait_ge(routed, 1)
            tr_begin("i")
            for w in range(2):
                for a in range(NT):
                    last = tp(ps[:, 6, w * T + a * P:w * T + (a + 1) * P], picked[:, w, a, :], ident)
            last.then_inc(tr_full, 1)
            tr_begin("g")
            for a in range(NT):
                last = tp(ps[:, 6, a * P:(a + 1) * P], vals[:, a].rearrange("p c k -> p (c k)"), ident)
            last.then_inc(tr_full, 1)
            with pe.Fori(NG // 8, NG // 4) as i:
                for s in range(4):
                    spread(s, i * 4 + s - NS)
                    u_group(s, i * 4 + s)

            def v_group(s, g, first=False, final=False):
                pe.wait_ge(alo_ready, g + 1)
                b = s % 2
                for j in range(GROUP):
                    pe.wait_ge(lo_ready, g * GROUP + NK + j + 1)
                    for a in range(NT):
                        ah, al = ahi[:, b, j, a * P:(a + 1) * P], alo[:, b, j, a * P:(a + 1) * P]
                        st, en = first and j == 0, final and j == GROUP - 1
                        for c in range(2):
                            o = ps[:, 2 + 2 * a + c, :]
                            mm(o, ah, whi[:, b, j, c * 512:(c + 1) * 512], start=st, stop=False)
                            mm(o, ah, wlo[:, b, j, c * 512:(c + 1) * 512], start=False, stop=False)
                            last = mm(o, al, whi[:, b, j, c * 512:(c + 1) * 512], start=False, stop=en)
                last.then_inc(group_full, 1)

            pe.wait_ge(s_done, 8)
            for s in range(4):
                spread(s, NS + s)
                v_group(s, s, first=(s == 0))
            with pe.Fori(1, NG // 8) as i:
                for s in range(4):
                    spread(s, i * 4 + s + NS)
                    v_group(s, i * 4 + s)
            with pe.Fori(NG // 8, NG // 4 - 1) as i:
                for s in range(4):
                    v_group(s, i * 4 + s)
            for s in range(4):
                v_group(s, NG - 4 + s, final=(s == 3))

        @block.scalar
        def _(act):
            act_fn = nc.scalar.activation
            count = [0]

            def link(ins):
                count[0] += 1
                ins.then_inc(act_done, 1)
                act.wait_ge(act_done, count[0])

            def signal(ins, s, value):
                ins.then_inc(s, 1)
                act.wait_ge(s, value)

            def evacuate(u):
                act.wait_ge(proj_full, u + 1)
                b = ps[:, u % 2, :]
                if u in (0, 1):
                    dst, src = fm_h[:, u, :], b
                elif u in (2, 3, 4, 5):
                    dst, src = tm[:, u % 2, (u // 4) * 512:(u // 4 + 1) * 512], b
                elif u in (6, 7):
                    dst, src = fm_m[:, 2 * (u - 6):2 * (u - 6) + 2, :].rearrange("p f t -> p (f t)"), b
                elif u == 8:
                    dst, src = fm_c.rearrange("p w t -> p (w t)"), b
                elif u == 9:
                    dst, src = rows[0:4, 3:5, :].rearrange("p w t -> p (w t)"), b[0:4, :]
                elif u == 10:
                    dst, src = tmg[:, :, 768:780], b[:, 0:24].rearrange("p (a n) -> p a n", a=NT)
                elif u in (11, 12, 13, 14):
                    a, c = (u - 11) % 2, (u - 11) // 2
                    dst, src = tmv[:, a, c * 512:(c + 1) * 512], b
                elif u in (15, 16):
                    dst, src = tmg[:, u - 15, 0:512], b
                elif u == 17:
                    dst, src = tmg[:, :, 512:768], b.rearrange("p (a n) -> p a n", a=NT)
                signal(act_fn(dst, src, ACT.Copy), proj_done, u + 1)

            def gate(i):
                u = N_PROJ + i
                act.wait_ge(proj_full, u + 1)
                m, k = ORDER[i // 4], 2 * (i % 4)
                signal(act_fn(gates[:, m, k:k + 2, :].rearrange("p k t -> p (k t)"), ps[:, u % 2, :],
                              ACT.Sigmoid), proj_done, u + 1)

            def hg_exp(li):
                if li < 8:
                    act.wait_ge(hg_d_ready, li)
                if li >= 3:
                    act.wait_ge(hg_qe_ready, li - 2)
                    act.wait_ge(hg_ke_ready, li - 2)
                L = LEVELS[li]
                e, d = hg_e[:, li % 2, :], hg_d[:, li % 2, :]
                if L < 64:
                    e4 = e.rearrange("p (b w l) -> p b w l", w=2, l=L)
                    d4 = d.rearrange("p (b w l) -> p b w l", w=2, l=L)
                    act_fn(e4[:, :, 0, :], d4[:, :, 0, :], ACT.Exp, scale=-1.0)
                    last = act_fn(e4[:, :, 1, :], d4[:, :, 1, :], ACT.Exp)
                elif L == 64:
                    e4 = e.rearrange("p (b w l) -> p b w l", w=2, l=L)
                    d4 = d.rearrange("p (b w l) -> p b w l", w=2, l=L)
                    b4 = hg_bc.rearrange("p (b w l) -> p b w l", w=2, l=L)
                    act_fn(e4[:, :, 0, :], d4[:, :, 0, :], ACT.Exp, scale=-1.0)
                    last = act_fn(e4[:, :, 1, :], b4[:, :, 1, :], ACT.Exp)
                else:
                    for f in range(2):
                        b, o = hg_bc[:, f * T:(f + 1) * T], e[:, f * T:(f + 1) * T]
                        act_fn(o[:, 0:64], b[:, 0:64], ACT.Exp, bias=hg_tot[:, f:f + 1], scale=-1.0)
                        act_fn(o[:, 64:128], b[:, 64:128], ACT.Exp, bias=b[:, 127:128], scale=-1.0)
                        act_fn(o[:, 128:192], b[:, 128:192], ACT.Exp)
                        last = act_fn(o[:, 192:256], b[:, 192:256], ACT.Exp, bias=b[:, 191:192])
                signal(last, hg_e_ready, li)

            def take_turned(name, dst, src=None, fn=ACT.Copy):
                act.wait_ge(tr_full, TR[name] + 1)
                signal(act_fn(dst, ps[:, 6, :] if src is None else src, fn), tr_taken, TR[name] + 1)

            def root(ready, at, dst, src, s):
                act.wait_ge(ready, at)
                signal(act_fn(dst, src, ACT.Sqrt), s, at)

            root(rms_ready, 1, small[:, 4:6], small[:, 2:4], root_ready)
            evacuate(0)
            link(act_fn(hg_t, fm_h[:, 0, :], ACT.Abs))
            link(act_fn(hg_t, hg_t, ACT.Exp, scale=-1.0))
            signal(act_fn(hg_t, hg_t, ACT.Ln, bias=1.0), hg_logs, 1)
            evacuate(1)
            act_fn(hg_qe[:, 0, :], fm_h[:, 1, :], ACT.Sigmoid)
            signal(act_fn(hg_k, fm_h[:, 0, :], ACT.Sigmoid, scale=-1.0), hg_sigs, 1)
            hg_exp(1)
            evacuate(2), evacuate(3)
            hg_exp(2), hg_exp(3)
            evacuate(4), evacuate(5)
            hg_exp(4), hg_exp(5)
            evacuate(6), evacuate(7)
            hg_exp(6), hg_exp(7), hg_exp(8)
            evacuate(8), evacuate(9), evacuate(10), evacuate(11), evacuate(12)
            root(qk_ms_ready, 1, r16, r16, qk_root)
            act.wait_ge(ml_f, 1)
            link(act_fn(rows[0:4, 2, :], rows[0:4, 4, :], ACT.Abs))
            link(act_fn(rows[0:4, 2, :], rows[0:4, 2, :], ACT.Exp, scale=-1.0))
            signal(act_fn(rows[0:4, 2, :], rows[0:4, 2, :], ACT.Ln, bias=1.0), ml_logs, 1)
            act.wait_ge(av_full, AV["hg"] + 1)
            signal(act_fn(sqb, ps[:, 7, :], ACT.Square), o_square, 1)
            for name in ("rq", "rk", "qrot", "q", "ks", "kw"):
                take_turned(name, attT[:, TR[name]].rearrange("p f t -> p (f t)"))
            root(o_ms, 1, r8, r8, o_root)
            evacuate(13), evacuate(14)
            act.wait_ge(av_full, AV["ret"] + 1)
            signal(act_fn(sqb, ps[:, 7, :], ACT.Square), o_square, 2)
            root(o_ms, 2, r8, r8, o_root)
            act.wait_ge(conv_done, 1)
            signal(act_fn(csg.rearrange("p f t -> p (f t)"), cv.rearrange("p f t -> p (f t)"), ACT.Sigmoid),
                   conv_sig, 1)
            act.wait_ge(tr_full, TR["mlgate"] + 1)
            link(act_fn(gcol, ps[:, 6, 0:8], ACT.Copy))
            signal(act_fn(enm, ps[:, 6, 8:16], ACT.Exp), tr_taken, TR["mlgate"] + 1)
            evacuate(15), evacuate(16), evacuate(17)
            act.wait_ge(ml_d_ready, 1)
            signal(act_fn(bufB, bufB, ACT.Exp), ml_e_ready, 1)
            signal(act_fn(sgb.rearrange("p a n -> p (a n)"), tmg.rearrange("p a n -> p (a n)"), ACT.Sigmoid),
                   sig_ready, 1)
            act.wait_ge(cmp_full, 1)
            for g in range(2):
                last = act_fn(kcs[:, :, g * HD:(g + 1) * HD],
                              ps[0:NCMP, 2 + g, 0:2 * HD].rearrange("p (w n) -> p w n", w=2), ACT.Copy)
            signal(last, cmp_out, 1)
            gate(0), gate(1)
            act.wait_ge(av_taken, AV["ml"] + 1)
            signal(act_fn(sqb, obuf[:, ML, :], ACT.Square), o_square, 3)
            root(o_ms, 3, r8, r8, o_root)
            root(kc_ms, 1, small[0:NCMP, 450:452], small[0:NCMP, 450:452], kc_root)
            act.wait_ge(tr_full, TR["kcmp"] + 1)
            signal(act_fn(kcT[:, 0:32].rearrange("p (g n) -> p g n", g=2)[:, :, 0:NCMP],
                          ps[:, 6, 0:32].rearrange("p (g n) -> p g n", g=2)[:, :, 0:NCMP], ACT.Copy),
                   tr_taken, TR["kcmp"] + 1)
            gate(2), gate(3)
            act.wait_ge(cs_ready, 1)
            signal(act_fn(cmpT, cmpS, ACT.Exp), ce_ready, 1)
            for a in range(NT):
                take_turned(f"pc{a}", pcT[:, a * 512:(a + 1) * 512], ps[0:NCMP, 6, :])

            def att_exps(n, a):
                act.wait_ge(att_max, n + 1)
                w = (a + 1) * P
                p = att_s[n % 2].rearrange("p (h n) -> p h n", h=H)
                for h in range(H):
                    last = act_fn(p[:, h, 0:w], p[:, h, 0:w], ACT.Exp, bias=nmx[:, n % 2, h:h + 1], scale=SCALE,
                                  accum_out=zsum[:, 1 + n // 2, a * H + h:a * H + h + 1])
                signal(last, att_exp, n + 1)

            def att_take(n, names):
                for s, name in enumerate(names):
                    take_turned(name, att_p[n % 2][:, s * 512:(s + 1) * 512])

            gate(4)
            att_exps(0, 0)
            gate(5)
            att_take(0, ["s0"])
            att_exps(1, 1)
            gate(6)
            att_take(1, ["s1a", "s1b"])
            gate(7)
            att_exps(2, 0)
            gate(8)

            def take_out(name, m):
                take_turned(name, outsT[:, m].rearrange("p f t -> p (f t)"))

            take_out("o3", RET), take_out("o0", HG)
            gate(9), gate(10)
            take_out("o1", ML)
            att_exps(3, 1)
            gate(11)
            act.wait_ge(av_full, AV["sel"] + 1)
            att_take(2, ["w0"])
            gate(12)
            att_take(3, ["w1a", "w1b"])
            gate(13), gate(14), gate(15)
            take_out("o2", NSA)
            root(rms_ready, 2, zs[:, 4:6], zs[:, 2:4], root_ready)
            act.wait_ge(xn_ready, 4)
            signal(act_fn(xhi.rearrange("p k t -> p (k t)"), xn2T.rearrange("p k t -> p (k t)"), ACT.Copy),
                   xhi_ready, 1)

            def high(s, at):
                act.wait_ge(u_loaded[s % 4], at)
                for j in range(GROUP):
                    act_fn(whi[:, s % 2, j], uring[:, s % 4, j], ACT.Copy).then_inc(hi_ready, 1)

            high(0, 16)
            high(1, 16)
            for u in range(8):
                act.wait_ge(q_full, u + 1)
                act_fn(qT[:, 2 * u:2 * u + 2, :].rearrange("p c t -> p (c t)"), ps[:, u % 2, :], ACT.Copy
                       ).then_inc(q_done, 1)
            for u in range(8):
                act.wait_ge(s_full, u + 1)
                act_fn(s_sb[:, u // 4, 4 * (u % 4):4 * (u % 4) + 4, :].rearrange("p c n -> p (c n)"),
                       ps[:, 2 + u % 4, :], ACT.Copy).then_inc(s_done, 1)

            def reload(table, load, s):
                act.dma_start(uring[:, s], table[bass.ds(load, 1)].rearrange("o p (j n) -> p (o j) n", j=GROUP)
                              ).then_inc(u_loaded[s], 16)

            def u_step(i, s, table=u_tab, skip=0):
                g = i * 4 + s
                act.wait_ge(group_full, g + 1)
                act_fn(hbuf[:, bass.ds(g * GROUP, GROUP), :].rearrange("p j t -> p (j t)"), ps[:, s % 2, :],
                       ACT.Gelu).then_inc(gelu_done, 1)
                high(s + 2, i * 16 + (16 if s < 2 else 32))
                act.wait_ge(lo_ready, g * GROUP + 2 * GROUP)
                reload(table, g + 1 + URING - skip, (s + 1) % URING)

            act.wait_ge(lo_ready, GROUP)
            reload(u_tab, URING, 0)
            with act.Fori(0, NG // 8) as i:
                for s in range(4):
                    u_step(i, s)
            act.wait_ge(vals_ready, 1)
            signal(act_fn(vals.rearrange("p a c k -> p (a c k)"), vals.rearrange("p a c k -> p (a c k)"),
                          ACT.Exp), g_exp, 1)
            act.wait_ge(tr_taken, TR["g"] + 1)
            with act.Fori(NG // 8, NG // 4 - 2) as i:
                for s in range(4):
                    u_step(i, s)
            for g in range(NG - 8, NG):
                late_ = g + 1 + URING >= NG
                u_step(g // 4, g % 4, v_tab if late_ else u_tab, NG if late_ else 0)

            def a_high(s, g):
                act_fn(ahi[:, s % 2].rearrange("p j t -> p (j t)"),
                       hbuf[:, bass.ds(g * GROUP, GROUP), :].rearrange("p j t -> p (j t)"), ACT.Copy
                       ).then_inc(ahi_ready, 1)

            act.wait_ge(g_taken, NS)
            a_high(0, 0)
            a_high(1, 1)

            def v_step(i, s, loads=True):
                g = i * 4 + s
                act.wait_ge(group_full, g + NG + 1)
                a_high(s, g + 2)
                high(s + 2, i * 16 + NG * 4 + (16 if s < 2 else 32))
                if loads:
                    act.wait_ge(lo_ready, g * GROUP + NK + 2 * GROUP)
                    reload(v_tab, g + 1 + URING, (s + 1) % URING)

            with act.Fori(0, NG // 8 - 1) as i:
                for s in range(4):
                    v_step(i, s)
            for s in range(4):
                if s == 2:
                    act.wait_ge(g_taken, 2 * NS)
                v_step(NG // 8 - 1, s)
            with act.Fori(NG // 8, NG // 4 - 2) as i:
                for s in range(4):
                    v_step(i, s)
            for g in range(NG - 8, NG - 2):
                v_step(g // 4, g % 4, loads=g + 1 + URING < NG)

        @block.vector
        def _(dve):
            v = nc.vector
            count = [0]

            def link(ins):
                count[0] += 1
                ins.then_inc(dve_done, 1)
                dve.wait_ge(dve_done, count[0])

            def signal(ins, s, value):
                ins.then_inc(s, 1)
                dve.wait_ge(s, value)

            def rms(n, xs, st, g, dst):
                for a in range(NT):
                    link(v.tensor_tensor_reduce(xs[:, a, :], xres[:, a, :], xres[:, a, :], 1.0, 0.0, ALU.mult,
                                                ALU.add, st[:, a:a + 1]))
                signal(v.tensor_scalar(st[:, 2:4], st[:, 0:2], 1.0 / D, EPS, ALU.mult, ALU.add),
                       rms_ready, n + 1)
                dve.wait_ge(root_ready, n + 1)
                link(v.reciprocal(st[:, 6:8], st[:, 4:6]))
                for a in range(NT):
                    signal(v.tensor_scalar(xs[:, a, :], xres[:, a, :], st[:, 6 + a:7 + a], None, ALU.mult),
                           xs_ready, 2 * n + a + 1)
                dve.wait_ge(xt_full, n + 1)
                for i in range(2):
                    signal(v.tensor_tensor(dst[:, 4 * i:4 * i + 4, :],
                                           ps[:, 2 + 2 * i:4 + 2 * i, :].rearrange("p b (k t) -> p (b k) t", k=2),
                                           bcast(g[:, 4 * i:4 * i + 4], T), ALU.mult), xn_ready, 2 * n + i + 1)

            def mean_squares(dst, src, n):
                link(v.tensor_reduce(dst, src, AX, ALU.add))
                return v.tensor_scalar(dst, dst, 1.0 / HD, EPS, ALU.mult, ALU.add)

            dve.wait_ge(x_loaded, 16)
            dve.wait_ge(consts_loaded, 64)
            rms(0, xs1, small, par("g1"), xnT)

            dve.wait_ge(hg_logs, 1)
            link(v.scalar_tensor_tensor(hg_d[:, 0, :], fm_h[:, 0, :], 0.0, hg_t, ALU.min, ALU.subtract))
            for f in range(2):
                c = slice(f * T, (f + 1) * T)
                link(v.tensor_tensor_scan(hg_bc[:, c], const("reset"), hg_d[:, 0, c], 0.0, ALU.mult, ALU.add))
            link(v.tensor_tensor(hg_tot, hg_bc[:, 63::256], hg_bc[:, 127::256], ALU.add))
            link(v.memset(hg_a, 0.0))
            dve.wait_ge(hg_sigs, 1)
            signal(v.tensor_tensor(hg_q, hg_qe[:, 0, :], fm_h[:, 1, :], ALU.mult), hg_q_ready, 1)

            def hg_diff(li):
                if li >= 3:
                    dve.wait_ge(hg_e_ready, li - 2)
                L = LEVELS[li]
                b4 = hg_bc.rearrange("p (b w l) -> p b w l", w=2, l=L)
                d4 = hg_d[:, li % 2, :].rearrange("p (b w l) -> p b w l", w=2, l=L)
                n = 512 // (2 * L)
                mid = b4[:, :, 0, L - 1:L].unsqueeze(2)
                if L < 64:
                    ins = v.tensor_tensor(d4, b4, mid.to_broadcast([P, n, 2, L]), ALU.subtract)
                else:
                    ins = v.tensor_tensor(d4[:, :, 0, :], b4[:, :, 0, :],
                                          b4[:, :, 0, L - 1:L].to_broadcast([P, n, L]), ALU.subtract)
                signal(ins, hg_d_ready, li)

            def hg_query(li):
                dve.wait_ge(hg_e_ready, li)
                if li >= 3:
                    dve.wait_ge(hg_full, li - 1)
                signal(v.tensor_tensor(hg_qe[:, li % 2, :], hg_e[:, li % 2, :], hg_q, ALU.mult),
                       hg_qe_ready, li)

            def hg_copy(li):
                dve.wait_ge(hg_full, li + 1)
                b = 2 + 2 * (li % 2)
                if LEVELS[li] == 128:
                    ins = v.tensor_copy(hg_off.rearrange("p (r n) -> p r n", r=2), ps[:, b:b + 2, 0:256])
                else:
                    mask = repeat(const("level")[:, li * P:(li + 1) * P].bitcast(U32), 4)
                    for r in range(2):
                        ins = v.copy_predicated(hg_a[:, 512 * r:512 * (r + 1)].rearrange("p (c n) -> p c n", c=4),
                                                mask, ps[:, b + r, :].rearrange("p (c n) -> p c n", c=4))
                        if r == 0:
                            link(ins)
                signal(ins, hg_copied, li + 1)

            hg_diff(1)
            hg_copy(0)
            for li in range(1, 9):
                if li < 7:
                    hg_diff(li + 1)
                hg_query(li)
                if li >= 2:
                    hg_copy(li - 1)
            hg_copy(8)

            nsa8 = tm[:, :, 512:1024]
            sq = obuf[:, 0:2, :]
            dve.wait_ge(proj_done, 6)
            link(v.tensor_tensor(sq, nsa8, nsa8, ALU.mult))
            signal(mean_squares(r16, sq.rearrange("p a (h n) -> p (a h) n", n=HD), 16), qk_ms_ready, 1)
            dve.wait_ge(proj_done, 10)
            gb = par("gb")
            R = rows[0:4]
            link(v.tensor_scalar(R[:, 3, :], R[:, 3, :], gb[0:4, 0:1], None, ALU.add))
            signal(v.tensor_scalar(R[:, 4, :], R[:, 4, :], gb[0:4, 1:2], None, ALU.add), ml_f, 1)
            dve.wait_ge(qk_root, 1)
            link(v.reciprocal(r16, r16))
            n4 = nsa8.rearrange("p a (h n) -> p a h n", n=HD)
            link(v.tensor_tensor(n4, n4, bcast(r16.rearrange("p (a h) -> p a h", a=NT), HD), ALU.mult))
            signal(v.tensor_tensor(nsa8, nsa8, repeat(par("gqk"), NT), ALU.mult), qk_normed, 1)
            cos4 = repeat(const("cos").rearrange("p (a n) -> p a n", a=NT), 16, axis=2)
            sin4 = repeat(const("sin").rearrange("p (a n) -> p a n", a=NT), 16, axis=2)
            x1, x2 = tmh[:, :, :, 0:32], tmh[:, :, :, 32:64]
            link(v.tensor_tensor(ropes[0], x1, cos4, ALU.mult))
            link(v.tensor_tensor(ropes[1], x2, sin4, ALU.mult))
            dve.wait_ge(rope_pool, 2)
            dve.wait_ge(qn_ready, 1)
            signal(v.tensor_tensor(x1, ropes[0], ropes[1], ALU.subtract), roped, 1)
            signal(v.tensor_tensor(x2, ropes[2], ropes[3], ALU.add), roped, 2)

            dve.wait_ge(ml_logs, 1)
            one4 = const("ones")[0:4, :]
            link(v.scalar_tensor_tensor(R[:, 0, :], R[:, 4, :], 0.0, R[:, 2, :], ALU.min, ALU.subtract))
            link(v.tensor_tensor_scan(R[:, 1, :], one4, R[:, 0, :], 0.0, ALU.mult, ALU.add))
            link(v.tensor_tensor(R[:, 5, :], R[:, 3, :], R[:, 1, :], ALU.subtract))
            link(v.tensor_tensor_scan(R[:, 6, :], one4, R[:, 5, :], 0.0, ALU.mult, ALU.max))
            link(v.tensor_scalar(R[:, 2, :], R[:, 6, :], -1.0, None, ALU.mult))
            signal(v.scalar_tensor_tensor(R[:, 0, :], R[:, 1, :], -1.0, R[:, 6, :], ALU.mult, ALU.subtract),
                   ml_rows, 1)
            dve.wait_ge(proj_done, 8)
            cw, cb = par("cw"), par("cb")
            for f in range(4):
                link(v.tensor_scalar(cv[:, f, :], fm_m[:, f, :], cw[:, 4 * f + 3:4 * f + 4], cb[:, f:f + 1],
                                     ALU.mult, ALU.add))
                for back in range(1, 4):
                    ins = v.scalar_tensor_tensor(cv[:, f, back:T], fm_m[:, f, 0:T - back],
                                                 cw[:, 4 * f + 3 - back:4 * f + 4 - back], cv[:, f, back:T],
                                                 ALU.mult, ALU.add)
                    if (f, back) != (3, 3):
                        link(ins)
            signal(ins, conv_done, 1)

            def out_norm(n, src, dst, gain):
                dve.wait_ge(o_square, n)
                signal(mean_squares(r8, head_norm(sqb), 8), o_ms, n)
                dve.wait_ge(o_root, n)
                link(v.reciprocal(r8, r8))
                ins = v.tensor_tensor(head_norm(dst), head_norm(src), bcast(r8, HD), ALU.mult)
                return ins

            def gain(dst, g):
                d3 = dst.rearrange("p (a n) -> p a n", a=NT)
                link(v.tensor_tensor(d3, d3, repeat(g, NT), ALU.mult))

            dve.wait_ge(tr_full, TR["kw"] + 1)
            signal(out_norm(1, ps[:, 7, :], obuf[:, HG, :], None), av_taken, 1)
            gain(obuf[:, HG, :], par("gh"))
            dve.wait_ge(ret_full, 1)
            signal(v.tensor_tensor(retA, ps[:, 2:6, 0:384],
                                   const("retd").rearrange("p (h n) -> p h n", h=H), ALU.mult), ret_a_ready, 1)
            signal(out_norm(2, ps[:, 7, :], obuf[:, RET, :], None), av_taken, 2)
            gain(obuf[:, RET, :], par("gr"))
            dve.wait_ge(conv_sig, 1)
            signal(v.tensor_tensor(cv, cv, csg, ALU.mult), conv_ready, 1)
            dve.wait_ge(tr_taken, TR["mlgate"] + 1)
            dve.wait_ge(ml_bc_full, 1)
            for h in range(H):
                c = (h % 2) * T
                link(v.tensor_scalar(mlW[:, h, 0:T], ps[:, 2 + h // 2, c:c + T], gcol[:, h:h + 1], 0.0,
                                     ALU.add, ALU.min))
                ins = v.tensor_scalar(mlW[:, h, T:T + P], ps[:, 2 + h // 2, c + P:c + T],
                                      gcol[:, 4 + h:5 + h], 0.0, ALU.add, ALU.min)
                if h < H - 1:
                    link(ins)
            signal(ins, ml_d_ready, 1)
            dve.wait_ge(ml_e_ready, 1)
            link(v.tensor_tensor(mlW, mlW, repeat(const("c01"), H), ALU.mult))
            dve.wait_ge(ml_full, 1)
            signal(v.tensor_tensor(mlW, mlW, ps[:, 2:6, 0:384], ALU.mult), ml_w_ready, 1)
            dve.wait_ge(sig_ready, 1)
            for c in (0, 512):
                link(v.tensor_tensor(sgb[:, :, c:c + 256], sgb[:, :, c:c + 256], tmg[:, :, c:c + 256], ALU.mult))

            def gated(m, c, at):
                o = obuf[:, m, :].rearrange("p (a n) -> p a n", a=NT)
                signal(v.tensor_tensor(o, o, sgb[:, :, c:c + 256], ALU.mult), o_ready, at)

            gated(RET, 512, 1)
            gated(HG, 0, 2)
            dve.wait_ge(cmp_out, 1)
            kr = small[0:NCMP, 450:452]
            ksq = sqb[0:NCMP, 0:128]
            link(v.tensor_tensor(ksq, kcs[:, 0, :], kcs[:, 0, :], ALU.mult))
            signal(mean_squares(kr, ksq.rearrange("p (g n) -> p g n", n=HD), 2), kc_ms, 1)
            dve.wait_ge(tr_full, TR["mlden"] + 1)
            den = small[:, 48:56]
            signal(v.tensor_copy(den, ps[:, 6, 0:8]), tr_taken, TR["mlden"] + 1)
            link(v.scalar_tensor_tensor(den, den, -1.0, den, ALU.mult, ALU.max))
            link(v.tensor_tensor(den, den, enm, ALU.max))
            link(v.reciprocal(den, den))
            dve.wait_ge(av_full, AV["ml"] + 1)
            signal(v.tensor_tensor(head_norm(obuf[:, ML, :]), head_norm(ps[:, 7, :]), bcast(den, HD), ALU.mult),
                   av_taken, 3)
            link(out_norm(3, obuf[:, ML, :], obuf[:, ML, :], None))
            gain(obuf[:, ML, :], par("gm"))
            gated(ML, 256, 3)
            dve.wait_ge(kc_root, 1)
            link(v.reciprocal(kr, kr))
            kv3 = kcs[:, 0, :].rearrange("p (g n) -> p g n", g=2)
            link(v.tensor_tensor(kv3, kv3, bcast(kr, HD), ALU.mult))
            k4 = kcn.rearrange("p (g r n) -> p g r n", g=2, r=2)
            signal(v.tensor_tensor(k4, repeat(kv3, 2, axis=2),
                                   repeat(par("gkc")[0:NCMP].rearrange("p (g n) -> p g n", g=2), 2, axis=2),
                                   ALU.mult), kc_ready, 1)
            dve.wait_ge(cs_full, 1)
            s4 = cmpS.rearrange("p (a h n) -> p a h n", a=NT, h=H)
            link(v.memset(cmpS, NEG))
            neg = const("cmpneg").rearrange("p (a n) -> p a n", a=NT)
            for a in range(NT):
                for r in range(2):
                    link(v.scalar_tensor_tensor(
                        s4[:, a, r::2, 0:NCMP],
                        ps[:, 4 + r, a * 32:a * 32 + 32].rearrange("p (f n) -> p f n", f=2)[:, :, 0:NCMP], SCALE,
                        repeat(neg[:, a, 0:NCMP], 2), ALU.mult, ALU.add))
            cmx = small[:, 56:64]
            s3 = cmpS.rearrange("p (g n) -> p g n", n=16)
            t3 = cmpT.rearrange("p (g n) -> p g n", n=16)
            link(v.tensor_reduce(cmx, s3[:, :, 0:NCMP], AX, ALU.max))
            signal(v.tensor_tensor(s3, s3, bcast(cmx, 16), ALU.subtract), cs_ready, 1)
            dve.wait_ge(ce_ready, 1)
            link(v.tensor_reduce(zsum[:, 0, :], t3[:, :, 0:NCMP], AX, ALU.add))
            t4 = cmpT.rearrange("p (a h n) -> p a h n", a=NT, h=H)
            signal(v.tensor_tensor(t4, t4, repeat(const("cmp01").rearrange("p (a n) -> p a n", a=NT), H, axis=2),
                                   ALU.mult), pc_ready, 1)

            def att_mask(n, a):
                dve.wait_ge(att_full, n + 1)
                if n >= 2:
                    dve.wait_ge(tr_full, TR["s0"] + 1 if n == 2 else TR["s1b"] + 1)
                b = 2 + 2 * (n % 2)
                p4 = att_s[n % 2].rearrange("p (f r n) -> p f r n", f=2, r=2)
                for r in range(2):
                    src = ps[:, b + r, :].rearrange("p (f n) -> p f n", f=2)
                    if a == 1:
                        link(v.tensor_copy(p4[:, :, r, 0:P], src[:, :, 0:P]))
                    link(v.tensor_tensor(p4[:, :, r, a * P:(a + 1) * P], src[:, :, a * P:(a + 1) * P],
                                         repeat(const("mneg"), 2), ALU.add))
                p3 = att_s[n % 2].rearrange("p (h n) -> p h n", h=H)
                link(v.tensor_reduce(nmx[:, n % 2, 0:4], p3[:, :, 0:(a + 1) * P], AX, ALU.max))
                signal(v.tensor_scalar(nmx[:, n % 2, 0:4], nmx[:, n % 2, 0:4], -SCALE, None, ALU.mult),
                       att_max, n + 1)

            def weigh(i, name, first):
                z = zsum[:, i, :]
                link(v.reciprocal(z, z))
                z4 = z.rearrange("p (a h) -> p a h", a=NT)
                link(v.tensor_tensor(z4, z4, sgb[:, :, 768 + i:780:3], ALU.mult))
                dve.wait_ge(av_full, AV[name] + 1)
                o = obuf[:, NSA, :] if first else sqb
                signal(v.tensor_tensor(head_norm(o), head_norm(ps[:, 7, :]), bcast(z, HD), ALU.mult),
                       av_taken, AV[name] + 1)

            att_mask(0, 0)
            weigh(0, "cmp", True)
            att_mask(1, 1)
            att_mask(2, 0)
            dve.wait_ge(att_exp, 2)
            weigh(1, "sel", False)
            link(v.tensor_tensor(obuf[:, NSA, :], obuf[:, NSA, :], sqb, ALU.add))
            att_mask(3, 1)
            dve.wait_ge(att_exp, 4)
            weigh(2, "win", False)
            signal(v.tensor_tensor(obuf[:, NSA, :], obuf[:, NSA, :], sqb, ALU.add), o_ready, 4)

            dve.wait_ge(proj_done, N_PROJ + N_GATE)
            for u in range(16):
                m, k = ORDER[u // 4], 2 * (u % 4)
                dve.wait_ge(up_full, u + 1)
                g = gates[:, m, k:k + 2, :].rearrange("p k t -> p (k t)")
                if u < 4:
                    dst = xnT[:, k:k + 2, :].rearrange("p k t -> p (k t)")
                else:
                    if u >= 7:
                        dve.wait_ge(up_add, u - 6)
                    dst = mtmp[:, u % 3, :]
                signal(v.tensor_tensor(dst, ps[:, u % 2, :], g, ALU.mult), up_mul, u + 1)
            for u in range(4):
                dve.wait_ge(y_full, u + 1)
                c, a = u // 2, u % 2
                signal(v.tensor_tensor(xres[:, a, c * 512:(c + 1) * 512], xres[:, a, c * 512:(c + 1) * 512],
                                       ps[:, u % 2, :], ALU.add), y_taken, u + 1)
            rms(1, xs2, zs, g2_sb, xn2T)
            dve.wait_ge(xhi_ready, 1)
            signal(v.tensor_tensor(xlo.rearrange("p k t -> p (k t)"), xn2T.rearrange("p k t -> p (k t)"),
                                   xhi.rearrange("p k t -> p (k t)"), ALU.subtract), xlo_ready, 1)
            link(v.tensor_copy(iota_bf, const("iota")))

            def top16(values, index, src, tmp):
                link(v.max(values[:, 0:8], src))
                link(v.max_index(index[:, 0:8], values[:, 0:8], src))
                link(v.match_replace(tmp, values[:, 0:8], src, GONE))
                link(v.max(values[:, 8:16], tmp))
                link(v.max_index(index[:, 8:16], values[:, 8:16], tmp))

            for a in range(NT):
                for c in range(16):
                    if c % 4 == 0:
                        dve.wait_ge(s_done, 4 * a + c // 4 + 1)
                    top16(v16[:, a, c, :], iu[:, a, c, :], s_sb[:, a, c, :], rep[:, 0, 0:NK])
            for a in range(NT):
                for h in range(PH):
                    link(v.tensor_tensor(cand.rearrange("p (i j) -> p i j", j=PK), bcast(v16[:, a, 2 * h, :], PK),
                                         repeat(v16[:, a, 2 * h + 1, :], PK), ALU.add))
                    top16(vals[:, a, h, :], pos[:, a, h, :], cand, rep[:, 1, :])
            link(v.tensor_tensor(vals[:, :, :, 1:PK], vals[:, :, :, 1:PK],
                                 vals[:, :, :, 0:1].to_broadcast([P, NT, PH, PK - 1]), ALU.subtract))
            signal(v.tensor_tensor(vals[:, :, :, 0:1], vals[:, :, :, 0:1], vals[:, :, :, 0:1], ALU.subtract),
                   vals_ready, 1)
            flat = lambda ap: ap.rearrange("p a c k -> p (a c k)")
            link(v.tensor_copy(flat(if_), flat(iu)))
            eq = rt_big.rearrange("p (c k j) -> p c k j", c=PH, k=PK)
            for w in range(2):
                if w == 0:
                    link(v.tensor_scalar(posr, flat(pos), 4, None, ALU.logical_shift_right))
                else:
                    link(v.tensor_scalar(posr, flat(pos), 15, None, ALU.bitwise_and))
                link(v.tensor_copy(posf, posr))
                for a in range(NT):
                    link(v.tensor_tensor(rt_big.rearrange("p (n j) -> p n j", j=PK),
                                         bcast(posf[:, a * 128:(a + 1) * 128], PK),
                                         repeat(const("iota16"), 128), ALU.is_equal))
                    link(v.tensor_tensor(eq, eq, repeat(if_[:, a, w::2, :], PK, axis=2), ALU.mult))
                    link(v.tensor_reduce(picked[:, w, a, :], rt_big.rearrange("p (n j) -> p n j", j=PK), AX,
                                         ALU.add))
            dve.wait_ge(g_exp, 1)
            z16 = zs[:, 8:24]
            v3 = vals.rearrange("p a c k -> p (a c) k")
            link(v.tensor_reduce(z16, v3, AX, ALU.add))
            link(v.reciprocal(z16, z16))
            signal(v.tensor_tensor(v3, v3, bcast(z16, PK), ALU.mult), routed, 1)
            dve.wait_ge(tr_full, TR["i"] + 1)
            link(v.tensor_copy(i1T, ps[:, 6, 0:T]))
            signal(v.tensor_copy(i2T, ps[:, 6, T:2 * T]), tr_taken, TR["i"] + 1)
            dve.wait_ge(tr_full, TR["g"] + 1)
            rounded = oh2[:, 0].rearrange("p t n -> p (t n)")[:, 0:T]
            link(v.tensor_copy(rounded, ps[:, 6, 0:T]))
            link(v.tensor_copy(ghT, rounded))
            signal(v.tensor_tensor(glT, ps[:, 6, 0:T], ghT, ALU.subtract), tr_taken, TR["g"] + 1)

            def one_hots(s, n, half):
                for t in range(TB):
                    c = bass.ds(n * TB + t, 1)
                    v.tensor_scalar(oh1h[:, s, t, :], iota_bf, i1T[:, c], ghT[:, c], ALU.is_equal, ALU.mult)
                    v.tensor_scalar(oh1l[:, s, t, :], iota_bf, i1T[:, c], glT[:, c], ALU.is_equal, ALU.mult)
                v.tensor_tensor(oh2[:, s], repeat(const("iota")[:, half * NJ:(half + 1) * NJ], TB),
                                bcast(i2T[:, bass.ds(n * TB, TB)], NJ), ALU.is_equal).then_inc(oh_ready, 1)

            def times_g(s, n, half):
                dve.wait_ge(g_full, n + half * NS + 1)
                h_ = hbuf[:, half * NJ:(half + 1) * NJ, bass.ds(n * TB, TB)]
                v.tensor_tensor(h_, h_, ps[:, 6 + s, :].rearrange("p (t j) -> p j t", t=TB), ALU.mult
                                ).then_inc(g_taken, 1)

            one_hots(0, 0, 0)
            dve.wait_ge(gelu_done, NG // 2)
            with dve.Fori(0, NS // 2 - 1) as i:
                for s in range(2):
                    one_hots(1 - s, i * 2 + s + 1, 0)
                    times_g(s, i * 2 + s, 0)
            one_hots(1, NS - 1, 0)
            times_g(0, NS - 2, 0)
            one_hots(0, 0, 1)
            times_g(1, NS - 1, 0)

            def a_low(s, g):
                dve.wait_ge(ahi_ready, g + 1)
                v.tensor_tensor(alo[:, s % 2].rearrange("p j t -> p (j t)"),
                                hbuf[:, bass.ds(g * GROUP, GROUP), :].rearrange("p j t -> p (j t)"),
                                ahi[:, s % 2].rearrange("p j t -> p (j t)"), ALU.subtract
                                ).then_inc(alo_ready, 1)

            a_low(0, 0)
            a_low(1, 1)

            def v_step(i, s, spreads=False):
                g = i * 2 + s
                if spreads:
                    one_hots(1 - s, g + 1, 1)
                    times_g(s, g, 1)
                dve.wait_ge(group_full, g + NG + 1)
                a_low(s, g + 2)

            dve.wait_ge(gelu_done, NG)
            with dve.Fori(0, NS // 2 - 1) as i:
                for s in range(2):
                    v_step(i, s, spreads=True)
            one_hots(1, NS - 1, 1)
            times_g(0, NS - 2, 1)
            times_g(1, NS - 1, 1)
            v_step(NS // 2 - 1, 0)
            v_step(NS // 2 - 1, 1)
            with dve.Fori(NS // 2, NG // 2 - 1) as i:
                for s in range(2):
                    v_step(i, s)
            dve.wait_ge(group_full, 2 * NG)
            for a in range(NT):
                v.tensor_tensor(xres[:, a, :].rearrange("p (c n) -> p c n", c=2),
                                xres[:, a, :].rearrange("p (c n) -> p c n", c=2),
                                ps[:, 2 + 2 * a:4 + 2 * a, :], ALU.add).then_inc(y2_ready, 1)

        @block.gpsimd
        def _(pool):
            g = nc.gpsimd
            for li in range(1, 9):
                pool.wait_ge(hg_e_ready, li)
                if li >= 3:
                    pool.wait_ge(hg_full, li - 1)
                g.tensor_tensor(hg_ke[:, li % 2, :], hg_e[:, li % 2, :], hg_k, ALU.mult).then_inc(hg_ke_ready, 1)
            pool.wait_ge(proj_done, 9)
            pool.wait_ge(consts_loaded, 64)
            for w in range(2):
                for half in range(2):
                    pe_ = par("pe")[:, w * CMPL + half * CMPS:w * CMPL + (half + 1) * CMPS]
                    g.tensor_tensor(kcp[:, w, half, :].rearrange("p (n l) -> p n l", l=CMPS),
                                    fm_c[:, w, :].rearrange("p (n l) -> p n l", l=CMPS), repeat(pe_, T // CMPS),
                                    ALU.add).then_inc(kcp_ready, 1)
            pool.wait_ge(qk_normed, 1)
            cos4 = repeat(const("cos").rearrange("p (a n) -> p a n", a=NT), 16, axis=2)
            sin4 = repeat(const("sin").rearrange("p (a n) -> p a n", a=NT), 16, axis=2)
            g.tensor_copy(qn, tm[:, :, 512:768]).then_inc(qn_ready, 1)
            g.tensor_tensor(ropes[2], tmh[:, :, :, 0:32], sin4, ALU.mult).then_inc(rope_pool, 1)
            g.tensor_tensor(ropes[3], tmh[:, :, :, 32:64], cos4, ALU.mult).then_inc(rope_pool, 1)
            pool.wait_ge(roped, 2)
            for a in range(NT):
                g.tensor_copy(kdup[:, a], repeat(tmh[:, a, 12:16, :], 2, axis=2)).then_inc(kdup_ready, 1)
            for u in range(4, 16):
                k = 2 * (u % 4)
                pool.wait_ge(up_mul, u + 1)
                o = xnT[:, k:k + 2, :].rearrange("p k t -> p (k t)")
                if u >= 8:
                    pool.wait_ge(up_add, u - 7)
                g.tensor_tensor(o, o, mtmp[:, u % 3, :], ALU.add).then_inc(up_add, 1)

            def low(s, at, hi_at):
                pool.wait_ge(u_loaded[s % 4], at)
                for j in range(GROUP):
                    pool.wait_ge(hi_ready, hi_at + j)
                    g.tensor_tensor(wlo[:, s % 2, j], uring[:, s % 4, j], whi[:, s % 2, j], ALU.subtract
                                    ).then_inc(lo_ready, 1)

            low(0, 16, 1)
            low(1, 16, GROUP + 1)

            def step(i, s):
                l = i * 4 + s
                pool.wait_ge(group_full, l + 1)
                low(s + 2, i * 16 + (16 if s < 2 else 32), l * GROUP + 2 * GROUP + 1)

            with pool.Fori(0, NG // 2 - 1) as i:
                for s in range(4):
                    step(i, s)
            step(NG // 2 - 1, 0)
            step(NG // 2 - 1, 1)


def kernel(x, norm1_g, w_in, hgrn_lb, hgrn_onorm_g, mlstm_conv_w, mlstm_conv_b, mlstm_gate_b,
           mlstm_onorm_g, nsa_qnorm_g, nsa_knorm_g, nsa_cmp_pe, nsa_cmp_w, ret_onorm_g, w_up,
           w_gate, w_out, norm2_g, peer_wq, peer_keys, peer_u, peer_v):
    import numpy as np
    import concourse.bacc as bacc
    from concourse.bass_utils import run_bass_kernel_spmd

    f = np.float32
    arr = lambda a: np.asarray(a)[0]

    def tiles(w):
        return np.ascontiguousarray(w.reshape(-1, P, w.shape[1]).transpose(1, 0, 2))

    def slot(w):
        t = tiles(w).reshape(P, -1)
        return t

    col, at = {}, 0
    for name, n in WIDTHS.items():
        col[name] = (at, at + n)
        at += n
    wi = arr(w_in)
    a_in = np.zeros((len(PROJ), P, KD, 512), wi.dtype)
    for s, names in enumerate(PROJ):
        part = tiles(np.concatenate([wi[:, col[n][0]:col[n][1]] for n in names], axis=1))
        a_in[s, :, :, :part.shape[2]] = part
    wc = arr(nsa_cmp_w).reshape(2, CMPL, HD, HD).transpose(2, 0, 1, 3).reshape(HD, -1)
    a_cmp = np.concatenate([wc, wc], axis=0)
    wg = arr(w_gate)
    a_gate = np.stack([slot(wg[m][:, c * 512:(c + 1) * 512]) for m in ORDER for c in range(2)])
    wu = arr(w_up)
    a_up = np.stack([np.concatenate([slot(wu[ORDER[2 * i + j]]) for j in range(2)], axis=1) for i in range(2)])
    wo = arr(w_out)
    a_out = np.stack([slot(wo[:, c * 512:(c + 1) * 512]) for c in range(2)])
    wqa = arr(peer_wq)
    a_wq = np.stack([slot(wqa[:, c * 512:(c + 1) * 512]) for c in range(4)])
    a_keys = np.ascontiguousarray(arr(peer_keys).reshape(16, NK, P).transpose(2, 0, 1).reshape(P, -1))
    ua = arr(peer_u).reshape(NK, NG, GROUP, KD, P)
    a_u = np.ascontiguousarray(ua.transpose(1, 4, 2, 3, 0)).reshape(NG, P, GROUP * D)
    va = arr(peer_v).reshape(NK, NG, GROUP, D)
    a_v = np.ascontiguousarray(va.transpose(1, 0, 2, 3)).reshape(NG, P, GROUP * D)

    i = np.arange(P)
    tri = (i[:, None] <= i[None, :]).astype(f)
    c = {}
    c["ident"] = np.eye(P, dtype=f)
    c["iota"] = np.broadcast_to(i.astype(f), (P, P))
    c["iota16"] = np.broadcast_to(np.arange(16, dtype=f), (P, 16))
    inv = 1.0 / (f(10000.0) ** (np.arange(0, HD, 2, dtype=f) / f(HD)))
    ang = (np.arange(T, dtype=f)[:, None] * inv[None, :].astype(f)).astype(f)
    by_tile = lambda t: t.reshape(NT, P, -1).transpose(1, 0, 2).reshape(P, -1).astype(f)
    c["cos"], c["sin"] = by_tile(np.cos(ang)), by_tile(np.sin(ang))
    c["mneg"] = np.where(tri.T > 0, 0.0, NEG).astype(f)
    c["c01"] = np.concatenate([tri, np.ones((P, P), f), tri], axis=1) * f(SCALE)
    lg = np.log1p(-np.exp2(-5.0 - np.arange(H)))
    diff = i[None, :] - i[:, None]
    retd = []
    for h in range(H):
        d0 = np.where(diff >= 0, np.exp(lg[h] * np.maximum(diff, 0)), 0.0)
        retd += [d0, np.exp(lg[h] * (diff + P)), d0]
    c["retd"] = (np.concatenate(retd, axis=1) * SCALE).astype(f)
    c["reset"] = np.broadcast_to((np.arange(T) % 64 != 0).astype(f), (P, T))
    c["ones"] = np.ones((P, T), f)
    blocks_end = np.arange(16) * CMPS + CMPL - 1
    ok = (blocks_end[None, :] <= np.arange(T)[:, None])
    ok[:, NCMP:] = False
    c["cmp01"] = by_tile(ok.astype(f))
    c["cmpneg"] = by_tile(np.where(ok, 0.0, NEG).astype(f))
    sel = np.zeros((P, H, P), f)
    for h in range(H):
        sel[h, h] = 1.0
    c["sel"] = sel.reshape(P, -1)
    lv = [np.eye(P, dtype=f)]
    for L in LEVELS[1:8]:
        b = i // (2 * L)
        lv.append(((b[:, None] == b[None, :]) & ((i % (2 * L) < L)[:, None]) & ((i % (2 * L) >= L)[None, :])
                   ).astype(f))
    c["level"] = np.concatenate(lv, axis=1)
    pack = lambda table, src: np.ascontiguousarray(np.concatenate([src[n].reshape(P, -1) for n in table], axis=1))
    a_late, a_front = pack(CONST_LATE, c).astype(f), pack(CONST_FRONT, c).astype(f)

    rep = lambda a: np.broadcast_to(a.reshape(1, -1), (P, a.size))
    p = {}
    p["g1"] = arr(norm1_g).reshape(KD, P).T
    cwa = arr(mlstm_conv_w)
    p["cw"] = cwa.reshape(4, 4, P).transpose(2, 1, 0).reshape(P, 16)
    p["cb"] = arr(mlstm_conv_b).reshape(4, P).T
    pea = arr(nsa_cmp_pe).transpose(2, 0, 1).reshape(HD, 2 * CMPL)
    p["pe"] = np.concatenate([pea, pea], axis=0)
    gb = np.zeros((P, 2), f)
    gb[0:4] = arr(mlstm_gate_b).reshape(2, 4).T
    p["gb"] = gb
    p["gh"], p["gm"], p["gr"] = rep(arr(hgrn_onorm_g)), rep(arr(mlstm_onorm_g)), rep(arr(ret_onorm_g))
    qn, kn = arr(nsa_qnorm_g), arr(nsa_knorm_g)
    p["gqk"] = rep(np.concatenate([qn] * 4 + [kn[1]] * 2 + [kn[2]] * 2))
    p["gkc"] = rep(np.concatenate([kn[0]] * 2))
    a_par = pack(PARAMS, p)
    a_g2 = np.ascontiguousarray(arr(norm2_g).reshape(KD, P).T)
    a_x = np.ascontiguousarray(arr(x).reshape(NT, P, D).transpose(1, 0, 2))

    arrays = dict(x=a_x, w_in=a_in.reshape(len(PROJ), P, SLOT), w_cmp=np.ascontiguousarray(a_cmp), w_gate=a_gate,
                  w_up=a_up, w_out=a_out, wq=a_wq, keys=a_keys, u_tab=a_u, v_tab=a_v, g2=a_g2,
                  late=a_late, front=a_front, params=a_par)
    nc = bacc.Bacc("TRN2", target_bir_lowering=False, num_devices=1)
    args = [nc.dram_tensor(f"in_{n}", a.shape, mybir.dt.from_np(a.dtype), kind="ExternalInput").ap()
            for n, a in arrays.items()]
    out = nc.dram_tensor("out", (T, D), F32, kind="ExternalOutput").ap()
    build(nc, *args, out)
    r = run_bass_kernel_spmd(nc, [{f"in_{n}": a for n, a in arrays.items()}], core_ids=[0])
    return r.results[0]["out"].reshape(1, T, D)
```

```python
from contextlib import ExitStack

import concourse.bass as bass
from concourse import mybir

F32 = mybir.dt.float32
BF16 = mybir.dt.bfloat16
U32 = mybir.dt.uint32
ALU = mybir.AluOpType
ACT = mybir.ActivationFunctionType
AX = mybir.AxisListType.X

P = 128
T = 256
NT = T // P
D = 1024
KD = D // P
H = 4
HD = 64
NCMP = 15
CMPL = 32
CMPS = 16
CMPR = 3 * 16 + NCMP
PH = 8
PK = 16
NK = 128
EPS = 1e-6
NEG = -1e30
GONE = -3e38
SCALE = HD ** -0.5
UNIT = 2048
WSLOTS = 3
GROUP = 2
NG = NK // GROUP
URING = 4
TB = 8
NJ = NK // 2
NS = T // TB

WIDTHS = dict(hq=256, hf=256, hi=256, hg=256, mq=256, mk=256, mv=256, mi=4, mf=4, mo=256, nq=256,
              kc=128, vc=128, ks=128, vs=128, kw=128, vw=128, ng=12, rq=256, rk=256, rv=256, rg=256)
PROJ = [("hf",), ("hq",), ("rq",), ("rk",), ("nq",), ("ks", "kw"), ("mq",), ("mk",), ("kc", "vc"),
        ("mi", 28, "mf", 28, "ng"), ("rv",), ("hi",), ("vs", "vw"), ("hg",), ("mv",), ("mo",), ("rg",)]
FEATURES = (0, 1, 6, 7, 8)
SMALL = 9
RET, HG, ML, NSA = 3, 0, 1, 2
ORDER = [RET, HG, ML, NSA]

CONST_LATE = dict(ident=128, iota=128, iota16=16)
CONST_FRONT = dict(cos=64, sin=64, mneg=128, c01=384, retd=1536, reset=256, ones=256, cmpneg=32,
                   cmp01=32, sel=512, level=1024)
PARAMS = dict(g1=8, cw=16, cb=4, pe=64, gb=2, gh=256, gm=256, gr=256, gqk=512, gkc=128)

N_PROJ = len(PROJ)
N_GATE = 16
GATE_UNIT = N_PROJ
UP_UNIT = GATE_UNIT + N_GATE
OUT_UNIT = UP_UNIT + 4
WQ_UNIT = OUT_UNIT + 4
N_UNITS = WQ_UNIT + 8
SPLIT = [6, 7, 12, 14, 15, *range(GATE_UNIT, UP_UNIT)]
LEVELS = [0, 1, 2, 4, 8, 16, 32, 64, 128]
TR = {n: i for i, n in enumerate(
    ["rq", "rk", "qrot", "q", "ks", "kw", "mlgate", "mlden", "kcmp", "pc0", "pc1",
     "s0", "s1a", "s1b", "o3", "o0", "o1", "w0", "w1a", "w1b", "o2", "i", "g"])}
AV = {n: i for i, n in enumerate(["hg", "ret", "ml", "cmp", "sel", "win"])}


def offsets(table):
    out, at = {}, 0
    for name, n in table.items():
        out[name] = (at, n)
        at += n
    return out, at


def bcast(ap, n):
    return ap.unsqueeze(ap.ndim).to_broadcast([*ap.shape, n])


def repeat(ap, n, axis=1):
    shape = [*ap.shape]
    shape.insert(axis, n)
    return ap.unsqueeze(axis).to_broadcast(shape)


def build(nc, x, w_in, w_cmp, w_gate, w_up, w_out, wq, keys, u_tab, v_tab, g2, late, front, params, out):
    off_late, n_late = offsets(CONST_LATE)
    off_front, n_front = offsets(CONST_FRONT)
    off_par, n_par = offsets(PARAMS)
    with ExitStack() as ctx:
        def sem(name):
            return ctx.enter_context(nc.semaphore(name))

        TOP = 53200
        arena = ctx.enter_context(nc.sbuf_tensor("arena", [P, TOP], F32))
        ps = ctx.enter_context(nc.psum_tensor("ps", [P, 8, 512], F32))

        class Region:
            def __init__(self, start, end):
                self.at, self.end = start, end

            def take(self, n):
                a = self.at
                self.at += n
                assert self.at <= self.end, (self.at, self.end)
                return arena[:, a:a + n]

        hbuf = arena[:, 0:NK * T].rearrange("p (j t) -> p j t", t=T)
        peer = Region(NK * T, TOP)
        uring = peer.take(URING * GROUP * D).rearrange("p (s j n) -> p s j n", s=URING, j=GROUP)
        whi = peer.take(GROUP * D).bitcast(BF16).rearrange("p (s j n) -> p s j n", s=2, j=GROUP)
        wlo = peer.take(GROUP * D).bitcast(BF16).rearrange("p (s j n) -> p s j n", s=2, j=GROUP)
        xhi = peer.take(D).bitcast(BF16).rearrange("p (k t) -> p k t", k=KD)
        xlo = peer.take(D).bitcast(BF16).rearrange("p (k t) -> p k t", k=KD)
        ahi = xhi.rearrange("p k t -> p (k t)")[:, 0:2 * GROUP * T].rearrange("p (s j t) -> p s j t", s=2, j=GROUP)
        alo = xlo.rearrange("p k t -> p (k t)")[:, 0:2 * GROUP * T].rearrange("p (s j t) -> p s j t", s=2, j=GROUP)
        i1T, i2T, ghT, glT = (peer.take(T) for _ in range(4))
        oh1, oh2h, oh2l = (peer.take(TB * n).bitcast(BF16).rearrange("p (s t n) -> p s t n", s=2, t=TB)
                           for n in (NK, NJ, NJ))
        eq2 = peer.take(TB * NJ // 2).bitcast(BF16).rearrange("p (t n) -> p t n", t=TB)
        top = peer.at
        xres = peer.take(NT * D).rearrange("p (a n) -> p a n", a=NT)
        late_sb = peer.take(n_late)
        g2_sb = peer.take(KD)
        rt = Region(16384, 32768)
        qT = arena[:, 12288:16384].rearrange("p (c t) -> p c t", t=T)
        xn2T = rt.take(KD * T).rearrange("p (k t) -> p k t", k=KD)
        rt_big = rt.take(2048)
        s_sb = rt.take(NT * 16 * NK).rearrange("p (a c n) -> p a c n", a=NT, c=16)
        rep = rt.take(2 * 256).rearrange("p (s n) -> p s n", s=2)
        cand = rt.take(256)
        v16 = rt.take(NT * 16 * PK).rearrange("p (a c k) -> p a c k", a=NT, c=16)
        iu = rt.take(NT * 16 * PK).bitcast(U32).rearrange("p (a c k) -> p a c k", a=NT, c=16)
        if_ = rt.take(NT * 16 * PK).rearrange("p (a c k) -> p a c k", a=NT, c=16)
        vals = rt.take(NT * PH * PK).rearrange("p (a c k) -> p a c k", a=NT, c=PH)
        pos = rt.take(NT * PH * PK).bitcast(U32).rearrange("p (a c k) -> p a c k", a=NT, c=PH)
        posr = rt.take(256).bitcast(U32)
        posf = rt.take(256)
        picked = rt.take(2 * 256).rearrange("p (w a n) -> p w a n", w=2, a=NT)
        zs = rt.take(32)
        fr = Region(0, top)
        wring = fr.take(WSLOTS * UNIT).rearrange("p (s n) -> p s n", s=WSLOTS)
        wparts = fr.take(WSLOTS * UNIT).bitcast(BF16).rearrange("p (s w n) -> p s w n", s=WSLOTS, w=2)
        gates_w = fr.take(4 * KD * T)
        gates = gates_w.rearrange("p (m k t) -> p m k t", m=4, k=KD)
        xn_place = fr.take(KD * T)
        xnp = xn_place.bitcast(BF16).rearrange("p (w k t) -> p w k t", w=2, k=KD)
        merged = xn_place.rearrange("p (k t) -> p k t", k=KD)
        outs_place = fr.take(4 * 2 * T)
        xn1 = outs_place.rearrange("p (k t) -> p k t", k=KD)
        outsT = outs_place.rearrange("p (m f t) -> p m f t", m=4, f=2)
        front_sb = fr.take(n_front)
        par_sb = fr.take(n_par)
        fm_h = fr.take(1024).rearrange("p (w n) -> p w n", w=2)
        fm_m = fr.take(1024).rearrange("p (f t) -> p f t", f=4)
        fm_c = fr.take(512).rearrange("p (w t) -> p w t", w=2)
        tm = fr.take(NT * 1024).rearrange("p (a n) -> p a n", a=NT)
        tmv = fr.take(NT * 1024).rearrange("p (a n) -> p a n", a=NT)
        tmg = fr.take(NT * 780).rearrange("p (a n) -> p a n", a=NT)
        attT = fr.take(6 * 512).rearrange("p (w f t) -> p w f t", w=6, f=2)
        bufA, bufB, bufC, bufD = (fr.take(n) for n in (1536, 1536, 1024, 1024))
        mtmp = bufA.rearrange("p (s n) -> p s n", s=3)
        obuf = fr.take(4 * 512).rearrange("p (m n) -> p m n", m=4)
        sqb = fr.take(512)
        small = fr.take(512)

        def const(name):
            o, n = (off_late if name in off_late else off_front)[name]
            return (late_sb if name in off_late else front_sb)[:, o:o + n]

        def par(name):
            o, n = off_par[name]
            return par_sb[:, o:o + n]

        ident = const("ident")
        xs1 = arena[:, 5 * UNIT:6 * UNIT].rearrange("p (a n) -> p a n", a=NT)
        xs2 = rt_big.rearrange("p (a n) -> p a n", a=NT)
        hgr = gates_w
        hg_bc = hgr[:, 0:512]
        hg_q, hg_k = hgr[:, 512:1024], hgr[:, 1024:1536]
        hg_d = hgr[:, 1536:2560].rearrange("p (s n) -> p s n", s=2)
        hg_e = hgr[:, 2560:3584].rearrange("p (s n) -> p s n", s=2)
        hg_qe = hgr[:, 3584:4608].rearrange("p (s n) -> p s n", s=2)
        hg_ke = hgr[:, 4608:5632].rearrange("p (s n) -> p s n", s=2)
        hg_a = hgr[:, 5632:6656]
        hg_off = hgr[:, 6656:7168]
        hg_t = hgr[:, 7168:7680]
        hg_tot = small[:, 16:18]
        kcp = [fm_h.rearrange("p w n -> p (w n)"), hgr[:, 7168:8192]]
        wcmp = hgr[:, 3072:7168].rearrange("p (l n) -> p l n", l=CMPL)
        ngT = obuf[:, RET, 0:T]
        cmpx = bufA[0:CMPR, 0:2 * HD]
        rows = hgr[:, 768:2560].rearrange("p (w t) -> p w t", w=7)
        sgb = tm.rearrange("p a n -> p (a n)")[:, 0:NT * 780].rearrange("p (a n) -> p a n", a=NT)
        ropes = [b[:, 0:1024].rearrange("p (a h n) -> p a h n", a=NT, h=16) for b in (bufA, bufB, bufC)]
        ropes.append(bufD[:, 0:1024].rearrange("p (a h n) -> p a h n", a=NT, h=16))
        r16 = small[:, 408:424]
        r8 = small[:, 440:448]
        kdup = obuf[:, 0:2, :].rearrange("p m n -> p (m n)").rearrange("p (a h r n) -> p a h r n", a=NT, h=4, r=2)
        qn = obuf[:, 2, :].rearrange("p (a n) -> p a n", a=NT)
        tmh = tm.rearrange("p a (h n) -> p a h n", n=HD)
        cv = bufC[:, 0:1024].rearrange("p (f t) -> p f t", f=4)
        csg = bufD[:, 0:1024].rearrange("p (f t) -> p f t", f=4)
        retA = bufA.rearrange("p (h n) -> p h n", h=H)
        mlW = bufB.rearrange("p (h n) -> p h n", h=H)
        gcol = small[:, 32:40]
        enm = small[:, 40:48]
        att_s = [bufA[:, 0:1024], bufB[:, 0:1024]]
        att_p = [bufC[:, 0:1024], bufD[:, 0:1024]]
        zsum = small[:, 64:88].rearrange("p (i n) -> p i n", i=3)
        nmx = small[:, 96:112].rearrange("p (i n) -> p i n", i=2)
        kcs = small[0:NCMP, 128:384].rearrange("p (w n) -> p w n", w=2)
        cmpS = sqb[:, 0:128]
        cmpT = sqb[:, 128:256]
        kcn = bufA[0:NCMP, 1024:1280]
        kcT = bufA[:, 1280:1312]
        pcT = bufB[0:NCMP, 0:1024]
        wslot = lambda n: wring[:, n % WSLOTS, :]
        wpart = lambda m, w: wparts[:, SPLIT.index(m) % WSLOTS, w, :]
        unit_size = lambda m: KD * 76 if m == SMALL else UNIT

        def head_norm(o):
            return o.rearrange("p (g n) -> p g n", n=HD)

        def scored(ap4):
            return ps[:, 2:6, 0:384]

        x_loaded, stored = [sem(f"x_loaded{a}") for a in range(NT)], sem("stored")
        late_loaded, front_loaded, params_loaded, g2_loaded = (sem("late_loaded"), sem("front_loaded"),
                                                               sem("params_loaded"), sem("g2_loaded"))
        w_loaded = [sem(f"w_loaded{i}") for i in range(WSLOTS)]
        u_loaded = [sem(f"u_loaded{i}") for i in range(URING)]
        dve_done, act_done, pool_done = sem("dve_done"), sem("act_done"), sem("pool_done")
        rms_ready, root_ready, xs_ready = sem("rms_ready"), sem("root_ready"), sem("xs_ready")
        xt_full, xn_ready = sem("xt_full"), sem("xn_ready")
        proj_full, proj_done = sem("proj_full"), sem("proj_done")
        hg_logs, hg_sigs, hg_q_ready = sem("hg_logs"), sem("hg_sigs"), sem("hg_q_ready")
        hg_d_ready, hg_e_ready = sem("hg_d_ready"), sem("hg_e_ready")
        hg_qe_ready, hg_ke_ready = sem("hg_qe_ready"), sem("hg_ke_ready")
        hg_full, hg_copied = sem("hg_full"), sem("hg_copied")
        qk_ms_ready, qk_root = sem("qk_ms_ready"), sem("qk_root")
        qk_normed, rope_pool, roped, kdup_ready, qn_ready = (sem("qk_normed"), sem("rope_pool"), sem("roped"),
                                                             sem("kdup_ready"), sem("qn_ready"))
        tr_full, tr_taken = sem("tr_full"), sem("tr_taken")
        av_full, av_taken = sem("av_full"), sem("av_taken")
        o_square, o_ms, o_root, o_ready = sem("o_square"), sem("o_ms"), sem("o_root"), sem("o_ready")
        ret_full, ret_a_ready = sem("ret_full"), sem("ret_a_ready")
        conv_done, conv_sig, conv_ready = sem("conv_done"), sem("conv_sig"), sem("conv_ready")
        ml_f, ml_logs, ml_rows = sem("ml_f"), sem("ml_logs"), sem("ml_rows")
        ml_bc_full, ml_d_ready, ml_e_ready, ml_full, ml_w_ready = (
            sem("ml_bc_full"), sem("ml_d_ready"), sem("ml_e_ready"), sem("ml_full"), sem("ml_w_ready"))
        sig_ready, gate_ready = sem("sig_ready"), sem("gate_ready")
        kcp_ready, cmp_full, cmp_out, kc_ms, kc_root, kc_ready = (
            sem("kcp_ready"), sem("cmp_full"), sem("cmp_out"), sem("kc_ms"), sem("kc_root"), sem("kc_ready"))
        cs_full, cs_ready, ce_ready, pc_ready = sem("cs_full"), sem("cs_ready"), sem("ce_ready"), sem("pc_ready")
        att_full, att_max, att_exp = sem("att_full"), sem("att_max"), sem("att_exp")
        up_full, up_mul, up_add = sem("up_full"), sem("up_mul"), sem("up_add")
        y_full, y_taken = sem("y_full"), sem("y_taken")
        xhi_ready, xlo_ready = sem("xhi_ready"), sem("xlo_ready")
        ng_turned, ng_taken = sem("ng_turned"), sem("ng_taken")
        whi_ready, wlo_ready = sem("whi_ready"), sem("wlo_ready")
        cmp_loaded, cmp_copied, cmp_sorted = sem("cmp_loaded"), sem("cmp_copied"), sem("cmp_sorted")
        q_full, q_done, s_full, s_done = sem("q_full"), sem("q_done"), sem("s_full"), sem("s_done")
        vals_ready, g_exp, routed = sem("vals_ready"), sem("g_exp"), sem("routed")
        hi_ready, lo_first, lo_ready = sem("hi_ready"), sem("lo_first"), sem("lo_ready")
        ahi_ready, alo_ready = sem("ahi_ready"), sem("alo_ready")
        group_full, gelu_done = sem("group_full"), sem("gelu_done")
        eq_ready = sem("eq_ready")
        oh_ready, g_full, g_taken, y2_full, y2_ready = (sem("oh_ready"), sem("g_full"), sem("g_taken"),
                                                        sem("y2_full"), sem("y2_ready"))

        stream = [(w_in[i], (proj_full, i + 1)) for i in range(N_PROJ)]
        stream += [(w_gate[i], (proj_full, N_PROJ + i + 1)) for i in range(N_GATE)]
        stream += [(w_up[i], (up_full, 4 * (i + 1))) for i in range(4)]
        stream += [(w_out[i], (y_full, i + 1)) for i in range(4)]
        stream += [(wq[i], (q_full, i + 1)) for i in range(8)]

        def wait_low(eng, m):
            eng.wait_ge(wlo_ready, SPLIT.index(m) + 1)

        def columns_low(eng, n):
            if isinstance(n, int) and n <= 2 * GROUP:
                eng.wait_ge(lo_first, n)
            else:
                eng.wait_ge(lo_ready, n - 2 * GROUP)

        block = ctx.enter_context(nc.Block())

        @block.sync
        def _(sp):
            for a in range(NT):
                sp.dma_start(xres[:, a, :], x[:, a, :]).then_inc(x_loaded[a], 16)
            sp.dma_start(late_sb, late).then_inc(late_loaded, 16)
            for n, (src, _) in enumerate(stream):
                if n >= WSLOTS:
                    if n - WSLOTS not in SPLIT:
                        sp.wait_ge(*stream[n - WSLOTS][1])
                    else:
                        wait_low(sp, n - WSLOTS)
                z = unit_size(n)
                sp.dma_start(wslot(n)[:, 0:z], src[:, 0:z]).then_inc(w_loaded[n % WSLOTS], 16)
                if n == 0:
                    sp.dma_start(par_sb, params).then_inc(params_loaded, 16)
                    sp.dma_start(front_sb, front).then_inc(front_loaded, 16)
                    sp.dma_start(g2_sb, g2).then_inc(g2_loaded, 16)
                if n == N_PROJ:
                    sp.wait_ge(av_full, AV["hg"] + 1)
                    sp.dma_start(wcmp.rearrange("p l n -> p (l n)"), w_cmp).then_inc(cmp_loaded, 16)
                if n == WQ_UNIT + 1:
                    sp.wait_ge(up_add, 12)
                    sp.wait_ge(up_mul, 16)
                    for s in range(URING):
                        sp.dma_start(uring[:, s], u_tab[s].rearrange("p (j n) -> p j n", j=GROUP)
                                     ).then_inc(u_loaded[s], 16)
            sp.wait_ge(*stream[N_UNITS - WSLOTS][1])
            sp.dma_start(wslot(N_UNITS), keys).then_inc(w_loaded[N_UNITS % WSLOTS], 16)

            for a in range(NT):
                sp.wait_ge(y2_ready, a + 1)
                sp.dma_start(out[a * P:(a + 1) * P, :], xres[:, a, :]).then_inc(stored, 16)
            sp.wait_ge(stored, 16 * NT)

        @block.tensor
        def _(pe):
            mm, tp = nc.tensor.matmul, nc.tensor.transpose

            def turn_x(src, ready_at):
                for a in range(NT):
                    pe.wait_ge(xs_ready, ready_at + a)
                    for k in range(KD):
                        last = tp(ps[:, 2 + k // 2, (k % 2) * T + a * P:(k % 2) * T + (a + 1) * P],
                                  src[:, a, k * P:(k + 1) * P], ident)
                last.then_inc(xt_full, 1)

            def mm3(o, sta, mov, start, stop):
                mm(o, sta[0], mov[0], start=start, stop=False)
                mm(o, sta[0], mov[1], start=False, stop=False)
                return mm(o, sta[1], mov[0], start=False, stop=stop)

            def parts(m):
                return [wpart(m, w).rearrange("p (k n) -> p k n", k=KD) for w in range(2)]

            xn_parts = [xnp[:, 0], xnp[:, 1]]

            def feature_tiles(bank, m, x, halves=None):
                w = wslot(m).rearrange("p (k n) -> p k n", k=KD) if m not in SPLIT else parts(m)
                for i in range(2):
                    for k in range(KD):
                        o, c = ps[:, bank, i * T:(i + 1) * T], slice(i * P, (i + 1) * P)
                        if halves is not None and i == 0 and k % 4 == 0:
                            pe.wait_ge(xn_ready, halves + k // 4 + 1)
                        if m in SPLIT:
                            last = mm3(o, [q[:, k, c] for q in w], [q[:, k, :] for q in x],
                                       start=(k == 0), stop=(k == KD - 1))
                        else:
                            last = mm(o, w[:, k, c], x[:, k, :], start=(k == 0), stop=(k == KD - 1))
                return last

            def token_tiles(bank, m, x, merging=False):
                w = wslot(m).rearrange("p (k n) -> p k n", k=KD) if m not in SPLIT else parts(m)
                for a in range(NT):
                    for k in range(KD):
                        o, c = ps[:, bank, a * 256:(a + 1) * 256], slice(a * P, (a + 1) * P)
                        if merging and a == 0 and k % 2 == 0:
                            pe.wait_ge(up_add, 9 + k // 2)
                        if m in SPLIT:
                            last = mm3(o, [q[:, k, c] for q in x], [q[:, k, :] for q in w],
                                       start=(k == 0), stop=(k == KD - 1))
                        else:
                            last = mm(o, x[:, k, c], w[:, k, :], start=(k == 0), stop=(k == KD - 1))
                return last

            def wait_unit(n):
                if n not in SPLIT:
                    pe.wait_ge(w_loaded[n % WSLOTS], 16 * (n // WSLOTS + 1))
                else:
                    wait_low(pe, n)

            def proj(u):
                wait_unit(u)
                if u >= 2:
                    pe.wait_ge(proj_done, u - 1)
                b = u % 2
                x = xn_parts if u in SPLIT else xn1
                if u == SMALL:
                    w = wslot(u)[:, 0:unit_size(u)].rearrange("p (k n) -> p k n", k=KD)
                    for k in range(KD):
                        last = mm(ps[0:76, b, 0:T], w[:, k, :], x[:, k, :], start=(k == 0), stop=(k == KD - 1))
                elif u in FEATURES:
                    last = feature_tiles(b, u, x, halves=0 if u == 0 else None)
                else:
                    last = token_tiles(b, u, x)
                last.then_inc(proj_full, 1)

            def gate(i):
                u = N_PROJ + i
                wait_low(pe, u)
                pe.wait_ge(proj_done, u - 1)
                feature_tiles(u % 2, u, xn_parts).then_inc(proj_full, 1)

            def hg_level(li):
                if li == 0:
                    pe.wait_ge(hg_sigs, 1)
                    pe.wait_ge(hg_q_ready, 1)
                    q, k = hg_q, hg_k
                else:
                    pe.wait_ge(hg_qe_ready, li)
                    pe.wait_ge(hg_ke_ready, li)
                    q, k = hg_qe[:, li % 2, :], hg_ke[:, li % 2, :]
                if li >= 2:
                    pe.wait_ge(hg_copied, li - 1)
                b = 2 + 2 * (li % 2)
                for f in range(2):
                    for par_ in range(2):
                        r = slice(64 * par_, 64 * par_ + 64)
                        if LEVELS[li] == 128:
                            last = mm(ps[:, b + par_, f * P:(f + 1) * P], k[r, f * T:f * T + P],
                                      q[r, f * T + P:f * T + T], start=True, stop=True)
                            continue
                        for st in range(2):
                            c = f * T + st * P
                            last = mm(ps[:, b + par_, c:c + P], k[r, c:c + P], q[r, c:c + P],
                                      start=True, stop=True)
                last.then_inc(hg_full, 1)

            def av(name, weights, values, blocks=None):
                n = AV[name]
                if n >= 1:
                    pe.wait_ge(av_taken, n)
                for a in range(NT):
                    for h in range(H):
                        parts = range(a + 1)
                        for s in parts:
                            last = mm(ps[:, 7, a * 256 + h * HD:a * 256 + (h + 1) * HD], weights(a, s, h),
                                      values(s, h), start=(s == 0), stop=(s == a))
                last.then_inc(av_full, 1)

            def tri(buf):
                return lambda a, s, h: buf[:, h, (a + s) * P:(a + s + 1) * P]

            def tr_begin(name):
                if TR[name]:
                    pe.wait_ge(tr_taken, TR[name])

            def turn_heads(name, src):
                tr_begin(name)
                for f in range(2):
                    for a in range(NT):
                        last = tp(ps[:, 6, f * T + a * P:f * T + (a + 1) * P], src(f, a), ident)
                last.then_inc(tr_full, 1)

            def full_scores(q, k, full):
                for h in range(H):
                    f, r = h // 2, slice(64 * (h % 2), 64 * (h % 2) + 64)
                    mm(ps[:, 2 + h, 0:T], k[r, f, 0:P], q[r, f, :], start=True, stop=True)
                    last = mm(ps[:, 2 + h, T:T + P], k[r, f, P:T], q[r, f, P:T], start=True, stop=True)
                last.then_inc(full, 1)

            def att_scores(n, which, a):
                b = 2 + 2 * (n % 2)
                if n >= 2:
                    pe.wait_ge(att_max, n - 1)
                for h in range(H):
                    f, r = h // 2, slice(64 * (h % 2), 64 * (h % 2) + 64)
                    w = (a + 1) * P
                    last = mm(ps[:, b + h % 2, f * T:f * T + w], attT[r, 2, f, a * P:(a + 1) * P],
                              attT[r, 4 + which, f, 0:w], start=True, stop=True)
                last.then_inc(att_full, 1)

            def att_turn(n, names, s0=0):
                pe.wait_ge(att_exp, n + 1)
                p = att_s[n % 2].rearrange("p (h n) -> p h n", h=H)
                for s, name in enumerate(names, s0):
                    tr_begin(name)
                    for h in range(H):
                        last = tp(ps[:, 6, h * P:(h + 1) * P], p[:, h, s * P:(s + 1) * P], ident)
                    last.then_inc(tr_full, 1)

            def att_av(name, n, a, taken):
                pe.wait_ge(tr_taken, taken)
                if a == 0:
                    pe.wait_ge(av_taken, AV[name])
                p = att_p[n % 2].rearrange("p (s h n) -> p s h n", s=2, h=H)
                c0 = 512 if name == "sel" else 640
                for h in range(H):
                    g = c0 - 0 + (h // 2) * HD
                    for s in range(a + 1):
                        last = mm(ps[:, 7, a * 256 + h * HD:a * 256 + (h + 1) * HD], p[:, s, h, :],
                                  tmv[:, s, g:g + HD], start=(s == 0), stop=(s == a))
                if a == 1:
                    last.then_inc(av_full, 1)

            def turn_out(name, m, ready_at):
                pe.wait_ge(o_ready, ready_at)
                turn_heads(name, lambda f, a: obuf[:, m, a * 256 + f * P:a * 256 + (f + 1) * P])

            pe.wait_ge(late_loaded, 16)
            turn_x(xs1, 1)
            proj(0), proj(1), proj(2), proj(3)
            hg_level(0)
            proj(4)
            hg_level(1), hg_level(2)
            proj(5), hg_level(3)
            proj(6), hg_level(4)
            proj(7), hg_level(5)
            proj(8), hg_level(6)
            proj(9), proj(10)
            pe.wait_ge(proj_done, SMALL + 1)
            for a in range(NT):
                last = tp(ps[:, 6, 12 * a:12 * a + 12], ngT[64:76, a * P:(a + 1) * P], ident[64:76, 64:76])
            last.then_inc(ng_turned, 1)
            hg_level(7), hg_level(8)
            proj(11)
            proj(12)
            pe.wait_ge(hg_copied, 9)
            pe.wait_ge(proj_done, 12)
            hg_a4 = hg_a.rearrange("p (r f s n) -> p r f s n", r=2, f=2, s=2)
            hg_off3 = hg_off.rearrange("p (r f n) -> p r f n", r=2, f=2)
            av("hg", lambda a, s, h: hg_off3[:, h % 2, h // 2, :] if a != s else hg_a4[:, h % 2, h // 2, a, :],
               lambda s, h: tmv[:, s, 256 + h * HD:256 + (h + 1) * HD])
            wait_unit(13)
            pe.wait_ge(proj_done, 12)
            w13 = wslot(13).rearrange("p (k n) -> p k n", k=KD)

            def piece(n):
                a, k0 = n // 2, KD // 2 * (n % 2)
                for k in range(k0, k0 + KD // 2):
                    last = mm(ps[:, 13 % 2, a * 256:(a + 1) * 256], xn1[:, k, a * P:(a + 1) * P], w13[:, k, :],
                              start=(k == 0), stop=(k == KD - 1))
                return last

            pe.wait_ge(roped, 2)
            pe.wait_ge(ng_taken, 1)
            for n, (name, c) in enumerate((("rq", 0), ("rk", 256), ("qrot", 512))):
                turn_heads(name, lambda f, a, c=c: tm[:, a, c + f * P:c + (f + 1) * P])
                piece(n)
            pe.wait_ge(qn_ready, 1)
            turn_heads("q", lambda f, a: qn[:, a, f * P:(f + 1) * P])
            piece(3).then_inc(proj_full, 1)
            pe.wait_ge(kdup_ready, 2)
            for w, name in enumerate(("ks", "kw")):
                turn_heads(name, lambda f, a, w=w: kdup[:, a, 2 * w + f].rearrange("p r n -> p (r n)"))
            pe.wait_ge(tr_taken, TR["rk"] + 1)
            full_scores(attT[:, 0], attT[:, 1], ret_full)
            proj(14)
            pe.wait_ge(ret_a_ready, 1)
            av("ret", tri(retA), lambda s, h: tmv[:, s, h * HD:(h + 1) * HD])
            pe.wait_ge(ml_rows, 1)
            tr_begin("mlgate")
            for i, r in enumerate((5, 0)):
                for a in range(NT):
                    last = tp(ps[:, 6, 8 * i + 4 * a:8 * i + 4 * a + 4], rows[0:4, r, a * P:(a + 1) * P],
                              ident[0:4, 0:4])
            last.then_inc(tr_full, 1)
            for h in range(H):
                last = mm(ps[:, 2 + h // 2, (h % 2) * T:(h % 2 + 1) * T], const("sel")[0:4, h * P:(h + 1) * P],
                          rows[0:4, 2, :], start=True, stop=True)
            last.then_inc(ml_bc_full, 1)
            proj(15), proj(16)
            pe.wait_ge(conv_ready, 1)
            pe.wait_ge(ml_d_ready, 1)
            full_scores(cv[:, 0:2], cv[:, 2:4], ml_full)
            pe.wait_ge(cmp_loaded, 16)
            pe.wait_ge(kcp_ready, 12)
            pe.wait_ge(av_taken, AV["ret"] + 1)
            for l in range(CMPL):
                at = l if l < CMPS else l % CMPS + CMPS
                last = mm(ps[0:CMPR, 7, 0:2 * HD], kcp[l // CMPS][:, at:at + CMPS * (CMPR - 1) + 1:CMPS],
                          wcmp[:, l, :], start=(l == 0), stop=(l == CMPL - 1))
            last.then_inc(cmp_full, 1)
            gate(0)
            pe.wait_ge(cmp_copied, 1)
            for w in range(2):
                for g in range(2):
                    c = T // CMPS * (2 * w + g)
                    last = mm(ps[0:NCMP, 7, 256 + (2 * w + g) * HD:256 + (2 * w + g + 1) * HD], ident[0:CMPR, c:c + NCMP],
                              cmpx[:, w * HD:(w + 1) * HD], start=True, stop=True)
            last.then_inc(cmp_sorted, 1)
            pe.wait_ge(ml_w_ready, 1)
            tr_begin("mlden")
            ones = const("ones")
            for a in range(NT):
                for h in range(H):
                    for s in range(a + 1):
                        last = mm(ps[:, 6, 4 * a + h:4 * a + h + 1], tri(mlW)(a, s, h), ones[:, 0:1],
                                  start=(s == 0), stop=(s == a))
            last.then_inc(tr_full, 1)
            pe.wait_ge(cmp_out, 1)
            av("ml", tri(mlW), lambda s, h: tmv[:, s, 768 + h * HD:768 + (h + 1) * HD])
            gate(1), gate(2)
            pe.wait_ge(kc_ready, 1)
            tr_begin("kcmp")
            for g in range(2):
                last = tp(ps[:, 6, g * 16:g * 16 + NCMP],
                          kcn.rearrange("p (g n) -> p g n", g=2)[:, g, :], ident[0:NCMP, 0:NCMP])
            last.then_inc(tr_full, 1)
            gate(3)
            pe.wait_ge(tr_taken, TR["kcmp"] + 1)
            for a in range(NT):
                for h in range(H):
                    f, r = h // 2, slice(64 * (h % 2), 64 * (h % 2) + 64)
                    last = mm(ps[:, 4 + h % 2, a * 32 + f * 16:a * 32 + f * 16 + NCMP],
                              attT[r, 3, f, a * P:(a + 1) * P], kcT[r, f * 16:f * 16 + NCMP],
                              start=True, stop=True)
            last.then_inc(cs_full, 1)
            gate(4)
            pe.wait_ge(pc_ready, 1)
            for a in range(NT):
                if a == 1:
                    pe.wait_ge(cs_ready, 1)
                    att_scores(0, 0, 0)
                tr_begin(f"pc{a}")
                for h in range(H):
                    c = (a * H + h) * 16
                    last = tp(ps[0:NCMP, 6, h * P:(h + 1) * P], cmpT[:, c:c + NCMP], ident)
                last.then_inc(tr_full, 1)
            gate(5)
            pe.wait_ge(tr_taken, TR["pc1"] + 1)
            pe.wait_ge(av_taken, AV["cmp"])
            for a in range(NT):
                for h in range(H):
                    last = mm(ps[:, 7, a * 256 + h * HD:a * 256 + (h + 1) * HD],
                              pcT[:, (a * H + h) * P:(a * H + h + 1) * P],
                              kcs[:, 1, (h // 2) * HD:(h // 2 + 1) * HD], start=True, stop=True)
            last.then_inc(av_full, 1)
            att_scores(1, 0, 1)
            gate(6)
            att_turn(0, ["s0"])
            gate(7)
            att_turn(1, ["s1a"])
            att_av("sel", 0, 0, TR["s0"] + 1)
            att_turn(1, ["s1b"], s0=1)
            att_scores(2, 1, 0)
            gate(8)
            att_av("sel", 1, 1, TR["s1b"] + 1)
            gate(9)
            turn_out("o3", RET, 1)
            gate(10)
            turn_out("o0", HG, 2)
            att_scores(3, 1, 1)
            gate(11)
            turn_out("o1", ML, 3)
            gate(12)
            att_turn(2, ["w0"])
            gate(13)
            att_turn(3, ["w1a"])
            att_av("win", 2, 0, TR["w0"] + 1)
            att_turn(3, ["w1b"], s0=1)
            gate(14)
            att_av("win", 3, 1, TR["w1b"] + 1)
            gate(15)

            def ups(i):
                m = ORDER[i]
                wait_unit(UP_UNIT + i)
                w = wslot(UP_UNIT + i).rearrange("p (k n) -> p k n", k=2)
                for c in range(4):
                    u = 4 * i + c
                    if u >= 2:
                        pe.wait_ge(up_mul, u - 1)
                    else:
                        pe.wait_ge(proj_done, N_PROJ + N_GATE - 1 + u)
                    for n in range(2):
                        for k in range(2):
                            col = (2 * c + n) * P
                            last = mm(ps[:, (u + 1) % 2, n * T:(n + 1) * T], w[:, k, col:col + P], outsT[:, m, k, :],
                                      start=(k == 0), stop=(k == 1))
                    last.then_inc(up_full, 1)

            pe.wait_ge(tr_taken, TR["o1"] + 1)
            ups(0)
            turn_out("o2", NSA, 4)
            ups(1), ups(2)
            pe.wait_ge(tr_taken, TR["o2"] + 1)
            ups(3)
            for q in range(4):
                wait_unit(OUT_UNIT + q)
                if q >= 2:
                    pe.wait_ge(y_taken, q - 1)
                else:
                    pe.wait_ge(up_mul, 15 + q)
                token_tiles((q + 1) % 2, OUT_UNIT + q, merged, merging=(q == 0)).then_inc(y_full, 1)
            turn_x(xs2, 3)
            pe.wait_ge(y_taken, 4)
            for u in range(8):
                wait_unit(WQ_UNIT + u)
                if u >= 2:
                    pe.wait_ge(q_done, u - 1)
                feature_tiles(u % 2, WQ_UNIT + u, xn2T, halves=2 if u == 0 else None).then_inc(q_full, 1)
            wait_unit(N_UNITS)
            kk = wslot(N_UNITS).rearrange("p (c n) -> p c n", c=16)
            for u in range(8):
                a, c4 = u // 4, u % 4
                if u >= 4:
                    pe.wait_ge(s_done, u - 3)
                else:
                    pe.wait_ge(q_done, 2 * c4 + 2)
                for c in range(4):
                    last = mm(ps[:, 2 + c4, c * NK:(c + 1) * NK], qT[:, 4 * c4 + c, a * P:(a + 1) * P],
                              kk[:, 4 * c4 + c, :], start=True, stop=True)
                last.then_inc(s_full, 1)
            pe.wait_ge(xlo_ready, 4)
            def u_group(s, g, gelus=True):
                if gelus:
                    pe.wait_ge(gelu_done, g - 1)
                for j in range(GROUP):
                    columns_low(pe, g * GROUP + j + 1)
                    for k in range(KD):
                        o = ps[:, s % 2, j * T:(j + 1) * T]
                        h_, l_ = whi[:, s % 2, j, k * P:(k + 1) * P], wlo[:, s % 2, j, k * P:(k + 1) * P]
                        mm(o, h_, xhi[:, k, :], start=(k == 0), stop=False)
                        mm(o, h_, xlo[:, k, :], start=False, stop=False)
                        last = mm(o, l_, xhi[:, k, :], start=False, stop=(k == KD - 1))
                last.then_inc(group_full, 1)

            def spread(s, n):
                pe.wait_ge(oh_ready, n + 1)
                for t in range(TB):
                    o = ps[:, 6 + s % 2, t * NJ:(t + 1) * NJ]
                    mm(o, oh1[:, s % 2, t, :], oh2h[:, s % 2, t, :], start=True, stop=False)
                    last = mm(o, oh1[:, s % 2, t, :], oh2l[:, s % 2, t, :], start=False, stop=True)
                last.then_inc(g_full, 1)

            for s in range(4):
                u_group(s, s, gelus=s >= 2)
            with pe.Fori(1, NG // 8 - 1) as i:
                for s in range(4):
                    u_group(s, i * 4 + s)
            pe.wait_ge(routed, 1)
            tr_begin("i")
            for w in range(2):
                for a in range(NT):
                    last = tp(ps[:, 6, w * T + a * P:w * T + (a + 1) * P], picked[:, w, a, :], ident)
            last.then_inc(tr_full, 1)
            tr_begin("g")
            for a in range(NT):
                last = tp(ps[:, 6, a * P:(a + 1) * P], vals[:, a].rearrange("p c k -> p (c k)"), ident)
            last.then_inc(tr_full, 1)
            for s in range(4):
                u_group(s, NG // 2 - 4 + s)
            with pe.Fori(NG // 8, NG // 4) as i:
                for s in range(4):
                    spread(s, i * 4 + s - NS)
                    u_group(s, i * 4 + s)

            def v_group(s, g, first=False):
                pe.wait_ge(alo_ready, g + 1)
                b = s % 2
                for j in range(GROUP):
                    columns_low(pe, g * GROUP + NK + j + 1)
                    for a in range(NT):
                        ah, al = ahi[:, b, j, a * P:(a + 1) * P], alo[:, b, j, a * P:(a + 1) * P]
                        st = first and j == 0
                        for c in range(2):
                            o = ps[:, 2 + 2 * a + c, :]
                            mm(o, ah, whi[:, b, j, c * 512:(c + 1) * 512], start=st, stop=False)
                            mm(o, ah, wlo[:, b, j, c * 512:(c + 1) * 512], start=False, stop=False)
                            last = mm(o, al, whi[:, b, j, c * 512:(c + 1) * 512], start=False, stop=False)
                last.then_inc(group_full, 1)

            pe.wait_ge(s_done, 8)
            for s in range(4):
                spread(s, NS + s)
                v_group(s, s, first=(s == 0))
            with pe.Fori(1, NG // 8) as i:
                for s in range(4):
                    spread(s, i * 4 + s + NS)
                    v_group(s, i * 4 + s)
            with pe.Fori(NG // 8, NG // 4 - 1) as i:
                for s in range(4):
                    v_group(s, i * 4 + s)
            for s in range(3):
                v_group(s, NG - 4 + s)
            pe.wait_ge(alo_ready, NG)
            columns_low(pe, 2 * NK)
            for a in range(NT):
                for j in range(GROUP):
                    ah, al = ahi[:, 1, j, a * P:(a + 1) * P], alo[:, 1, j, a * P:(a + 1) * P]
                    for c in range(2):
                        o = ps[:, 2 + 2 * a + c, :]
                        mm(o, ah, whi[:, 1, j, c * 512:(c + 1) * 512], start=False, stop=False)
                        mm(o, ah, wlo[:, 1, j, c * 512:(c + 1) * 512], start=False, stop=False)
                        last = mm(o, al, whi[:, 1, j, c * 512:(c + 1) * 512], start=False, stop=(j == GROUP - 1))
                last.then_inc(y2_full, 1)

        @block.scalar
        def _(act):
            act_fn = nc.scalar.activation
            count = [0]

            def link(ins):
                count[0] += 1
                ins.then_inc(act_done, 1)
                act.wait_ge(act_done, count[0])

            def signal(ins, s, value):
                ins.then_inc(s, 1)
                act.wait_ge(s, value)

            def w_high(m):
                act.wait_ge(w_loaded[m % WSLOTS], 16 * (m // WSLOTS + 1))
                n = SPLIT.index(m)
                if n >= WSLOTS:
                    done, value = stream[SPLIT[n - WSLOTS]][1]
                    act.wait_ge(done, value)
                elif n == WSLOTS - 1:
                    act.wait_ge(xt_full, 1)
                act_fn(wpart(m, 0), wslot(m), ACT.Copy).then_inc(whi_ready, 1)

            def x_high(n, dst, src):
                for i in range(2):
                    act.wait_ge(xn_ready, 2 * n + i + 1)
                    act_fn(dst[:, 4 * i:4 * i + 4, :], src[:, 4 * i:4 * i + 4, :], ACT.Copy
                           ).then_inc(xhi_ready, 1)

            def evacuate(u):
                act.wait_ge(proj_full, u + 1)
                b = ps[:, u % 2, :]
                by_token = b.rearrange("p (a n) -> p a n", a=NT)
                if u in (0, 1):
                    dst, src = fm_h[:, u, :], b
                elif u in (2, 3, 4, 5):
                    dst, src = tm[:, :, (u - 2) * 256:(u - 1) * 256], by_token
                elif u in (6, 7):
                    dst, src = fm_m[:, 2 * (u - 6):2 * (u - 6) + 2, :].rearrange("p f t -> p (f t)"), b
                elif u == 8:
                    dst, src = fm_c.rearrange("p w t -> p (w t)"), b
                elif u == SMALL:
                    act_fn(rows[0:4, 3, :], b[0:4, 0:T], ACT.Copy)
                    act_fn(rows[0:4, 4, :], b[32:36, 0:T], ACT.Copy)
                    dst, src = ngT[64:76, :], b[64:76, 0:T]
                elif u in (10, 11, 12, 14):
                    c = {10: 0, 11: 256, 12: 512, 14: 768}[u]
                    dst, src = tmv[:, :, c:c + 256], by_token
                elif u in (13, 15, 16):
                    c = {13: 0, 15: 256, 16: 512}[u]
                    dst, src = tmg[:, :, c:c + 256], by_token
                signal(act_fn(dst, src, ACT.Copy), proj_done, u + 1)
                for m in {4: [6], 5: [7], 10: [12], 14: [17], 15: [18]}.get(u, []):
                    w_high(m)

            def gate(i, high_too=True):
                u = N_PROJ + i
                act.wait_ge(proj_full, u + 1)
                m, k = ORDER[i // 4], 2 * (i % 4)
                signal(act_fn(gates[:, m, k:k + 2, :].rearrange("p k t -> p (k t)"), ps[:, u % 2, :],
                              ACT.Sigmoid), proj_done, u + 1)
                if high_too and u + WSLOTS in SPLIT:
                    w_high(u + WSLOTS)

            def hg_exp(li):
                if li < 8:
                    act.wait_ge(hg_d_ready, li)
                if li >= 3:
                    act.wait_ge(hg_qe_ready, li - 2)
                    act.wait_ge(hg_ke_ready, li - 2)
                L = LEVELS[li]
                e, d = hg_e[:, li % 2, :], hg_d[:, li % 2, :]
                if L < 64:
                    e4 = e.rearrange("p (b w l) -> p b w l", w=2, l=L)
                    d4 = d.rearrange("p (b w l) -> p b w l", w=2, l=L)
                    act_fn(e4[:, :, 0, :], d4[:, :, 0, :], ACT.Exp, scale=-1.0)
                    last = act_fn(e4[:, :, 1, :], d4[:, :, 1, :], ACT.Exp)
                elif L == 64:
                    e4 = e.rearrange("p (b w l) -> p b w l", w=2, l=L)
                    d4 = d.rearrange("p (b w l) -> p b w l", w=2, l=L)
                    b4 = hg_bc.rearrange("p (b w l) -> p b w l", w=2, l=L)
                    act_fn(e4[:, :, 0, :], d4[:, :, 0, :], ACT.Exp, scale=-1.0)
                    last = act_fn(e4[:, :, 1, :], b4[:, :, 1, :], ACT.Exp)
                else:
                    for f in range(2):
                        b, o = hg_bc[:, f * T:(f + 1) * T], e[:, f * T:(f + 1) * T]
                        act_fn(o[:, 0:64], b[:, 0:64], ACT.Exp, bias=hg_tot[:, f:f + 1], scale=-1.0)
                        act_fn(o[:, 64:128], b[:, 64:128], ACT.Exp, bias=b[:, 127:128], scale=-1.0)
                        act_fn(o[:, 128:192], b[:, 128:192], ACT.Exp)
                        last = act_fn(o[:, 192:256], b[:, 192:256], ACT.Exp, bias=b[:, 191:192])
                signal(last, hg_e_ready, li)

            def take_turned(name, dst, src=None, fn=ACT.Copy):
                act.wait_ge(tr_full, TR[name] + 1)
                signal(act_fn(dst, ps[:, 6, :] if src is None else src, fn), tr_taken, TR[name] + 1)

            def root(ready, at, dst, src, s):
                act.wait_ge(ready, at)
                signal(act_fn(dst, src, ACT.Sqrt), s, at)

            act.wait_ge(late_loaded, 16)
            act_fn(small[:, 8:9], ident[:, 0:1], ACT.Sqrt)
            root(rms_ready, 1, small[:, 4:6], small[:, 2:4], root_ready)
            x_high(0, xnp[:, 0], xn1)
            evacuate(0)
            link(act_fn(hg_t, fm_h[:, 0, :], ACT.Abs))
            link(act_fn(hg_t, hg_t, ACT.Exp, scale=-1.0))
            signal(act_fn(hg_t, hg_t, ACT.Ln, bias=1.0), hg_logs, 1)
            evacuate(1)
            act_fn(hg_qe[:, 0, :], fm_h[:, 1, :], ACT.Sigmoid)
            signal(act_fn(hg_k, fm_h[:, 0, :], ACT.Sigmoid, scale=-1.0), hg_sigs, 1)
            hg_exp(1)
            for li in range(2, 9):
                evacuate(li)
                hg_exp(li)
            evacuate(9)
            root(qk_ms_ready, 1, r16, r16, qk_root)
            evacuate(10)
            act.wait_ge(ng_turned, 1)
            signal(act_fn(tmg[:, :, 768:780], ps[:, 6, 0:24].rearrange("p (a n) -> p a n", a=NT), ACT.Copy),
                   ng_taken, 1)
            evacuate(11)
            act.wait_ge(ml_f, 1)
            link(act_fn(rows[0:4, 2, :], rows[0:4, 4, :], ACT.Abs))
            link(act_fn(rows[0:4, 2, :], rows[0:4, 2, :], ACT.Exp, scale=-1.0))
            signal(act_fn(rows[0:4, 2, :], rows[0:4, 2, :], ACT.Ln, bias=1.0), ml_logs, 1)
            evacuate(12)
            act.wait_ge(av_full, AV["hg"] + 1)
            signal(act_fn(sqb, ps[:, 7, :], ACT.Square), o_square, 1)
            for name in ("rq", "rk", "qrot", "q", "ks", "kw"):
                take_turned(name, attT[:, TR[name]].rearrange("p f t -> p (f t)"))
                if name == "rk":
                    w_high(14)
            w_high(15)
            evacuate(13)
            root(o_ms, 1, r8, r8, o_root)
            evacuate(14)
            act.wait_ge(av_full, AV["ret"] + 1)
            signal(act_fn(sqb, ps[:, 7, :], ACT.Square), o_square, 2)
            root(o_ms, 2, r8, r8, o_root)
            act.wait_ge(conv_done, 1)
            signal(act_fn(csg.rearrange("p f t -> p (f t)"), cv.rearrange("p f t -> p (f t)"), ACT.Sigmoid),
                   conv_sig, 1)
            act.wait_ge(tr_full, TR["mlgate"] + 1)
            link(act_fn(gcol, ps[:, 6, 0:8], ACT.Copy))
            signal(act_fn(enm, ps[:, 6, 8:16], ACT.Exp), tr_taken, TR["mlgate"] + 1)
            evacuate(15), evacuate(16)
            act.wait_ge(ml_d_ready, 1)
            signal(act_fn(bufB, bufB, ACT.Exp), ml_e_ready, 1)
            signal(act_fn(sgb.rearrange("p a n -> p (a n)"), tmg.rearrange("p a n -> p (a n)"), ACT.Sigmoid),
                   sig_ready, 1)
            w_high(19)
            act.wait_ge(cmp_full, 1)
            signal(act_fn(cmpx, ps[0:CMPR, 7, 0:2 * HD], ACT.Copy), cmp_copied, 1)
            gate(0)
            act.wait_ge(cmp_sorted, 1)
            signal(act_fn(kcs.rearrange("p w n -> p (w n)"), ps[0:NCMP, 7, 256:256 + 4 * HD], ACT.Copy), cmp_out, 1)
            root(kc_ms, 1, small[0:NCMP, 450:452], small[0:NCMP, 450:452], kc_root)
            gate(1), gate(2)
            act.wait_ge(av_taken, AV["ml"] + 1)
            signal(act_fn(sqb, obuf[:, ML, :], ACT.Square), o_square, 3)
            act.wait_ge(tr_full, TR["kcmp"] + 1)
            signal(act_fn(kcT[:, 0:32].rearrange("p (g n) -> p g n", g=2)[:, :, 0:NCMP],
                          ps[:, 6, 0:32].rearrange("p (g n) -> p g n", g=2)[:, :, 0:NCMP], ACT.Copy),
                   tr_taken, TR["kcmp"] + 1)
            root(o_ms, 3, r8, r8, o_root)
            gate(3)
            act.wait_ge(cs_ready, 1)
            signal(act_fn(cmpT, cmpS, ACT.Exp), ce_ready, 1)
            gate(4, high_too=False)
            for a in range(NT):
                take_turned(f"pc{a}", pcT[:, a * 512:(a + 1) * 512], ps[0:NCMP, 6, :])
            w_high(GATE_UNIT + 4 + WSLOTS)

            def att_exps(n, a):
                act.wait_ge(att_max, n + 1)
                w = (a + 1) * P
                p = att_s[n % 2].rearrange("p (h n) -> p h n", h=H)
                for h in range(H):
                    last = act_fn(p[:, h, 0:w], p[:, h, 0:w], ACT.Exp, bias=nmx[:, n % 2, h:h + 1], scale=SCALE,
                                  accum_out=zsum[:, 1 + n // 2, a * H + h:a * H + h + 1])
                signal(last, att_exp, n + 1)

            def att_take(n, names):
                for s, name in enumerate(names):
                    take_turned(name, att_p[n % 2][:, s * 512:(s + 1) * 512])

            gate(5)
            att_exps(0, 0)
            att_exps(1, 1)
            gate(6)
            att_take(0, ["s0"])
            gate(7, high_too=False)
            att_take(1, ["s1a", "s1b"])
            w_high(GATE_UNIT + 7 + WSLOTS)
            gate(8)
            att_exps(2, 0)
            gate(9)

            def take_out(name, m):
                take_turned(name, outsT[:, m].rearrange("p f t -> p (f t)"))

            take_out("o3", RET)
            gate(10)
            take_out("o0", HG)
            gate(11)
            take_out("o1", ML)
            att_exps(3, 1)
            gate(12)
            act.wait_ge(av_full, AV["sel"] + 1)
            att_take(2, ["w0"])
            gate(13)
            att_take(3, ["w1a", "w1b"])
            gate(14), gate(15)
            take_out("o2", NSA)
            act_fn(small[:, 9:10], ident[:, 0:1], ACT.Sqrt)
            root(rms_ready, 2, zs[:, 4:6], zs[:, 2:4], root_ready)
            x_high(1, xhi, xn2T)

            def high(s, at):
                act.wait_ge(u_loaded[s % 4], at)
                for j in range(GROUP):
                    act_fn(whi[:, s % 2, j], uring[:, s % 4, j], ACT.Copy).then_inc(hi_ready, 1)

            high(0, 16)
            high(1, 16)
            for u in range(8):
                act.wait_ge(q_full, u + 1)
                act_fn(qT[:, 2 * u:2 * u + 2, :].rearrange("p c t -> p (c t)"), ps[:, u % 2, :], ACT.Copy
                       ).then_inc(q_done, 1)
            for u in range(8):
                act.wait_ge(s_full, u + 1)
                act_fn(s_sb[:, u // 4, 4 * (u % 4):4 * (u % 4) + 4, :].rearrange("p c n -> p (c n)"),
                       ps[:, 2 + u % 4, :], ACT.Copy).then_inc(s_done, 1)

            def reload(table, load, s):
                act.dma_start(uring[:, s], table[bass.ds(load, 1)].rearrange("o p (j n) -> p (o j) n", j=GROUP)
                              ).then_inc(u_loaded[s], 16)

            def u_step(i, s, table=u_tab, skip=0, last=False):
                g = i * 4 + s
                act.wait_ge(group_full, g + 1)
                act_fn(hbuf[:, bass.ds(g * GROUP, GROUP), :].rearrange("p j t -> p (j t)"), ps[:, s % 2, :],
                       ACT.Gelu).then_inc(gelu_done, 1)
                if last:
                    act.wait_ge(g_taken, NS)
                    a_high(0, 0)
                high(s + 2, i * 16 + (16 if s < 2 else 32))
                columns_low(act, g * GROUP + 2 * GROUP)
                reload(table, g + 1 + URING - skip, (s + 1) % URING)

            columns_low(act, GROUP)
            reload(u_tab, URING, 0)
            for s in range(4):
                u_step(0, s)
            with act.Fori(1, NG // 8 - 2) as i:
                for s in range(4):
                    u_step(i, s)
            act.wait_ge(vals_ready, 1)
            signal(act_fn(vals.rearrange("p a c k -> p (a c k)"), vals.rearrange("p a c k -> p (a c k)"),
                          ACT.Exp), g_exp, 1)
            with act.Fori(NG // 8 - 2, NG // 8) as i:
                for s in range(4):
                    u_step(i, s)
            act.wait_ge(tr_taken, TR["g"] + 1)
            with act.Fori(NG // 8, NG // 4 - 2) as i:
                for s in range(4):
                    u_step(i, s)
            def a_high(s, g):
                act_fn(ahi[:, s % 2].rearrange("p j t -> p (j t)"),
                       hbuf[:, bass.ds(g * GROUP, GROUP), :].rearrange("p j t -> p (j t)"), ACT.Copy
                       ).then_inc(ahi_ready, 1)

            for g in range(NG - 8, NG):
                from_v = g + 1 + URING >= NG
                u_step(g // 4, g % 4, v_tab if from_v else u_tab, NG if from_v else 0, last=(g == NG - 1))
            a_high(1, 1)

            def v_step(i, s, loads=True):
                g = i * 4 + s
                act.wait_ge(group_full, g + NG + 1)
                a_high(s, g + 2)
                high(s + 2, i * 16 + NG * 4 + (16 if s < 2 else 32))
                if loads:
                    columns_low(act, g * GROUP + NK + 2 * GROUP)
                    reload(v_tab, g + 1 + URING, (s + 1) % URING)

            with act.Fori(0, NG // 8 - 1) as i:
                for s in range(4):
                    v_step(i, s)
            for s in range(4):
                if s == 2:
                    act.wait_ge(g_taken, 2 * NS)
                v_step(NG // 8 - 1, s)
            with act.Fori(NG // 8, NG // 4 - 2) as i:
                for s in range(4):
                    v_step(i, s)
            for g in range(NG - 8, NG - 2):
                v_step(g // 4, g % 4, loads=g + 1 + URING < NG)

        @block.vector
        def _(dve):
            v = nc.vector
            count = [0]

            def link(ins):
                count[0] += 1
                ins.then_inc(dve_done, 1)
                dve.wait_ge(dve_done, count[0])

            def signal(ins, s, value):
                ins.then_inc(s, 1)
                dve.wait_ge(s, value)

            def rms(n, xs, st, g, dst, high, low):
                if n == 0:
                    for a in range(NT):
                        dve.wait_ge(x_loaded[a], 16)
                        link(v.tensor_tensor_reduce(xs[:, a, :], xres[:, a, :], xres[:, a, :], 1.0, 0.0, ALU.mult,
                                                    ALU.add, st[:, a:a + 1]))
                else:
                    link(v.tensor_reduce(st[:, 0:2], st[:, 24:32].rearrange("p (a q) -> p a q", a=NT), AX, ALU.add))
                signal(v.tensor_scalar(st[:, 2:4], st[:, 0:2], 1.0 / D, EPS, ALU.mult, ALU.add),
                       rms_ready, n + 1)
                dve.wait_ge(root_ready, n + 1)
                link(v.reciprocal(st[:, 6:8], st[:, 4:6]))
                for a in range(NT):
                    signal(v.tensor_scalar(xs[:, a, :], xres[:, a, :], st[:, 6 + a:7 + a], None, ALU.mult),
                           xs_ready, 2 * n + a + 1)
                dve.wait_ge(xt_full, n + 1)
                dve.wait_ge(g2_loaded if n else params_loaded, 16)
                for i in range(2):
                    signal(v.tensor_tensor(dst[:, 4 * i:4 * i + 4, :],
                                           ps[:, 2 + 2 * i:4 + 2 * i, :].rearrange("p b (k t) -> p (b k) t", k=2),
                                           bcast(g[:, 4 * i:4 * i + 4], T), ALU.mult), xn_ready, 2 * n + i + 1)
                for i in range(2):
                    dve.wait_ge(xhi_ready, 2 * n + i + 1)
                    c = slice(4 * i, 4 * i + 4)
                    signal(v.tensor_tensor(low[:, c, :], dst[:, c, :], high[:, c, :], ALU.subtract),
                           xlo_ready, 2 * n + i + 1)

            def mean_squares(dst, src, n):
                link(v.tensor_reduce(dst, src, AX, ALU.add))
                return v.tensor_scalar(dst, dst, 1.0 / HD, EPS, ALU.mult, ALU.add)

            rms(0, xs1, small, par("g1"), xn1, xnp[:, 0], xnp[:, 1])

            dve.wait_ge(front_loaded, 16)
            dve.wait_ge(hg_logs, 1)
            link(v.scalar_tensor_tensor(hg_d[:, 0, :], fm_h[:, 0, :], 0.0, hg_t, ALU.min, ALU.subtract))
            for f in range(2):
                c = slice(f * T, (f + 1) * T)
                link(v.tensor_tensor_scan(hg_bc[:, c], const("reset"), hg_d[:, 0, c], 0.0, ALU.mult, ALU.add))
            link(v.tensor_tensor(hg_tot, hg_bc[:, 63::256], hg_bc[:, 127::256], ALU.add))
            link(v.memset(hg_a, 0.0))
            dve.wait_ge(hg_sigs, 1)
            signal(v.tensor_tensor(hg_q, hg_qe[:, 0, :], fm_h[:, 1, :], ALU.mult), hg_q_ready, 1)

            def hg_diff(li):
                if li >= 3:
                    dve.wait_ge(hg_e_ready, li - 2)
                L = LEVELS[li]
                b4 = hg_bc.rearrange("p (b w l) -> p b w l", w=2, l=L)
                d4 = hg_d[:, li % 2, :].rearrange("p (b w l) -> p b w l", w=2, l=L)
                n = 512 // (2 * L)
                mid = b4[:, :, 0, L - 1:L].unsqueeze(2)
                if L < 64:
                    ins = v.tensor_tensor(d4, b4, mid.to_broadcast([P, n, 2, L]), ALU.subtract)
                else:
                    ins = v.tensor_tensor(d4[:, :, 0, :], b4[:, :, 0, :],
                                          b4[:, :, 0, L - 1:L].to_broadcast([P, n, L]), ALU.subtract)
                signal(ins, hg_d_ready, li)

            def hg_query(li):
                dve.wait_ge(hg_e_ready, li)
                if li >= 3:
                    dve.wait_ge(hg_full, li - 1)
                signal(v.tensor_tensor(hg_qe[:, li % 2, :], hg_e[:, li % 2, :], hg_q, ALU.mult),
                       hg_qe_ready, li)
                signal(v.tensor_tensor(hg_ke[:, li % 2, :], hg_e[:, li % 2, :], hg_k, ALU.mult),
                       hg_ke_ready, li)

            def hg_copy(li):
                dve.wait_ge(hg_full, li + 1)
                b = 2 + 2 * (li % 2)
                if LEVELS[li] == 128:
                    ins = v.tensor_copy(hg_off.rearrange("p (r n) -> p r n", r=2), ps[:, b:b + 2, 0:256])
                else:
                    mask = repeat(const("level")[:, li * P:(li + 1) * P].bitcast(U32), 4)
                    for r in range(2):
                        ins = v.copy_predicated(hg_a[:, 512 * r:512 * (r + 1)].rearrange("p (c n) -> p c n", c=4),
                                                mask, ps[:, b + r, :].rearrange("p (c n) -> p c n", c=4))
                        if r == 0:
                            link(ins)
                signal(ins, hg_copied, li + 1)

            hg_diff(1)
            hg_copy(0)
            nsa8 = tm[:, :, 512:1024]
            sq = obuf[:, 0:2, :]
            for li in range(1, 9):
                if li < 7:
                    hg_diff(li + 1)
                hg_query(li)
                if li == 8:
                    dve.wait_ge(qk_root, 1)
                    link(v.reciprocal(r16, r16))
                    n4 = nsa8.rearrange("p a (h n) -> p a h n", n=HD)
                    link(v.tensor_tensor(n4, n4, bcast(r16.rearrange("p (a h) -> p a h", a=NT), HD), ALU.mult))
                    signal(v.tensor_tensor(nsa8, nsa8, repeat(par("gqk"), NT), ALU.mult), qk_normed, 1)
                if li >= 2:
                    hg_copy(li - 1)
                if li == 7:
                    dve.wait_ge(proj_done, 6)
                    link(v.tensor_tensor(sq, nsa8, nsa8, ALU.mult))
                    signal(mean_squares(r16, sq.rearrange("p a (h n) -> p (a h) n", n=HD), 16), qk_ms_ready, 1)
            hg_copy(8)

            dve.wait_ge(proj_done, 10)
            gb = par("gb")
            R = rows[0:4]
            link(v.tensor_scalar(R[:, 3, :], R[:, 3, :], gb[0:4, 0:1], None, ALU.add))
            signal(v.tensor_scalar(R[:, 4, :], R[:, 4, :], gb[0:4, 1:2], None, ALU.add), ml_f, 1)
            cos4 = repeat(const("cos").rearrange("p (a n) -> p a n", a=NT), 16, axis=2)
            sin4 = repeat(const("sin").rearrange("p (a n) -> p a n", a=NT), 16, axis=2)
            x1, x2 = tmh[:, :, :, 0:32], tmh[:, :, :, 32:64]
            link(v.tensor_tensor(ropes[0], x1, cos4, ALU.mult))
            link(v.tensor_tensor(ropes[1], x2, sin4, ALU.mult))
            dve.wait_ge(rope_pool, 2)
            dve.wait_ge(qn_ready, 1)
            signal(v.tensor_tensor(x1, ropes[0], ropes[1], ALU.subtract), roped, 1)
            signal(v.tensor_tensor(x2, ropes[2], ropes[3], ALU.add), roped, 2)

            dve.wait_ge(ml_logs, 1)
            one4 = const("ones")[0:4, :]
            link(v.scalar_tensor_tensor(R[:, 0, :], R[:, 4, :], 0.0, R[:, 2, :], ALU.min, ALU.subtract))
            link(v.tensor_tensor_scan(R[:, 1, :], one4, R[:, 0, :], 0.0, ALU.mult, ALU.add))
            link(v.tensor_tensor(R[:, 5, :], R[:, 3, :], R[:, 1, :], ALU.subtract))
            link(v.tensor_tensor_scan(R[:, 6, :], one4, R[:, 5, :], 0.0, ALU.mult, ALU.max))
            link(v.tensor_scalar(R[:, 2, :], R[:, 6, :], -1.0, None, ALU.mult))
            signal(v.scalar_tensor_tensor(R[:, 0, :], R[:, 1, :], -1.0, R[:, 6, :], ALU.mult, ALU.subtract),
                   ml_rows, 1)
            dve.wait_ge(proj_done, 8)
            cw, cb = par("cw"), par("cb")
            for f in range(4):
                link(v.tensor_scalar(cv[:, f, :], fm_m[:, f, :], cw[:, 4 * f + 3:4 * f + 4], cb[:, f:f + 1],
                                     ALU.mult, ALU.add))
                for back in range(1, 4):
                    ins = v.scalar_tensor_tensor(cv[:, f, back:T], fm_m[:, f, 0:T - back],
                                                 cw[:, 4 * f + 3 - back:4 * f + 4 - back], cv[:, f, back:T],
                                                 ALU.mult, ALU.add)
                    if (f, back) != (3, 3):
                        link(ins)
            signal(ins, conv_done, 1)

            def out_norm(n, src, dst, gain):
                dve.wait_ge(o_square, n)
                signal(mean_squares(r8, head_norm(sqb), 8), o_ms, n)
                dve.wait_ge(o_root, n)
                link(v.reciprocal(r8, r8))
                ins = v.tensor_tensor(head_norm(dst), head_norm(src), bcast(r8, HD), ALU.mult)
                return ins

            def gain(dst, g):
                d3 = dst.rearrange("p (a n) -> p a n", a=NT)
                link(v.tensor_tensor(d3, d3, repeat(g, NT), ALU.mult))

            dve.wait_ge(tr_full, TR["kw"] + 1)
            signal(out_norm(1, ps[:, 7, :], obuf[:, HG, :], None), av_taken, 1)
            gain(obuf[:, HG, :], par("gh"))
            dve.wait_ge(ret_full, 1)
            signal(v.tensor_tensor(retA, ps[:, 2:6, 0:384],
                                   const("retd").rearrange("p (h n) -> p h n", h=H), ALU.mult), ret_a_ready, 1)
            signal(out_norm(2, ps[:, 7, :], obuf[:, RET, :], None), av_taken, 2)
            gain(obuf[:, RET, :], par("gr"))
            dve.wait_ge(conv_sig, 1)
            signal(v.tensor_tensor(cv, cv, csg, ALU.mult), conv_ready, 1)
            dve.wait_ge(tr_taken, TR["mlgate"] + 1)
            dve.wait_ge(ml_bc_full, 1)
            for h in range(H):
                c = (h % 2) * T
                link(v.tensor_scalar(mlW[:, h, 0:T], ps[:, 2 + h // 2, c:c + T], gcol[:, h:h + 1], 0.0,
                                     ALU.add, ALU.min))
                ins = v.tensor_scalar(mlW[:, h, T:T + P], ps[:, 2 + h // 2, c + P:c + T],
                                      gcol[:, 4 + h:5 + h], 0.0, ALU.add, ALU.min)
                if h < H - 1:
                    link(ins)
            signal(ins, ml_d_ready, 1)
            dve.wait_ge(ml_e_ready, 1)
            link(v.tensor_tensor(mlW, mlW, repeat(const("c01"), H), ALU.mult))
            dve.wait_ge(ml_full, 1)
            signal(v.tensor_tensor(mlW, mlW, ps[:, 2:6, 0:384], ALU.mult), ml_w_ready, 1)
            dve.wait_ge(sig_ready, 1)
            for c in (0, 512):
                link(v.tensor_tensor(sgb[:, :, c:c + 256], sgb[:, :, c:c + 256], tmg[:, :, c:c + 256], ALU.mult))

            def gated(m, c, at):
                o = obuf[:, m, :].rearrange("p (a n) -> p a n", a=NT)
                signal(v.tensor_tensor(o, o, sgb[:, :, c:c + 256], ALU.mult), o_ready, at)

            gated(RET, 512, 1)
            gated(HG, 0, 2)
            dve.wait_ge(cmp_out, 1)
            kr = small[0:NCMP, 450:452]
            ksq = sqb[0:NCMP, 0:128]
            link(v.tensor_tensor(ksq, kcs[:, 0, :], kcs[:, 0, :], ALU.mult))
            signal(mean_squares(kr, ksq.rearrange("p (g n) -> p g n", n=HD), 2), kc_ms, 1)
            dve.wait_ge(kc_root, 1)
            link(v.reciprocal(kr, kr))
            kv3 = kcs[:, 0, :].rearrange("p (g n) -> p g n", g=2)
            link(v.tensor_tensor(kv3, kv3, bcast(kr, HD), ALU.mult))
            k4 = kcn.rearrange("p (g r n) -> p g r n", g=2, r=2)
            signal(v.tensor_tensor(k4, repeat(kv3, 2, axis=2),
                                   repeat(par("gkc")[0:NCMP].rearrange("p (g n) -> p g n", g=2), 2, axis=2),
                                   ALU.mult), kc_ready, 1)
            dve.wait_ge(tr_full, TR["mlden"] + 1)
            den = small[:, 48:56]
            signal(v.tensor_copy(den, ps[:, 6, 0:8]), tr_taken, TR["mlden"] + 1)
            link(v.scalar_tensor_tensor(den, den, -1.0, den, ALU.mult, ALU.max))
            link(v.tensor_tensor(den, den, enm, ALU.max))
            link(v.reciprocal(den, den))
            dve.wait_ge(av_full, AV["ml"] + 1)
            signal(v.tensor_tensor(head_norm(obuf[:, ML, :]), head_norm(ps[:, 7, :]), bcast(den, HD), ALU.mult),
                   av_taken, 3)
            link(out_norm(3, obuf[:, ML, :], obuf[:, ML, :], None))
            gain(obuf[:, ML, :], par("gm"))
            gated(ML, 256, 3)
            dve.wait_ge(cs_full, 1)
            s4 = cmpS.rearrange("p (a h n) -> p a h n", a=NT, h=H)
            link(v.memset(cmpS, NEG))
            neg = const("cmpneg").rearrange("p (a n) -> p a n", a=NT)
            for a in range(NT):
                for r in range(2):
                    link(v.scalar_tensor_tensor(
                        s4[:, a, r::2, 0:NCMP],
                        ps[:, 4 + r, a * 32:a * 32 + 32].rearrange("p (f n) -> p f n", f=2)[:, :, 0:NCMP], SCALE,
                        repeat(neg[:, a, 0:NCMP], 2), ALU.mult, ALU.add))
            cmx = small[:, 56:64]
            s3 = cmpS.rearrange("p (g n) -> p g n", n=16)
            t3 = cmpT.rearrange("p (g n) -> p g n", n=16)
            link(v.tensor_reduce(cmx, s3[:, :, 0:NCMP], AX, ALU.max))
            signal(v.tensor_tensor(s3, s3, bcast(cmx, 16), ALU.subtract), cs_ready, 1)
            dve.wait_ge(ce_ready, 1)
            link(v.tensor_reduce(zsum[:, 0, :], t3[:, :, 0:NCMP], AX, ALU.add))
            t4 = cmpT.rearrange("p (a h n) -> p a h n", a=NT, h=H)
            signal(v.tensor_tensor(t4, t4, repeat(const("cmp01").rearrange("p (a n) -> p a n", a=NT), H, axis=2),
                                   ALU.mult), pc_ready, 1)

            def att_mask(n, a):
                dve.wait_ge(att_full, n + 1)
                if n >= 2:
                    dve.wait_ge(tr_full, TR["s0"] + 1 if n == 2 else TR["s1b"] + 1)
                b = 2 + 2 * (n % 2)
                p4 = att_s[n % 2].rearrange("p (f r n) -> p f r n", f=2, r=2)
                for r in range(2):
                    src = ps[:, b + r, :].rearrange("p (f n) -> p f n", f=2)
                    if a == 1:
                        link(v.tensor_copy(p4[:, :, r, 0:P], src[:, :, 0:P]))
                    link(v.tensor_tensor(p4[:, :, r, a * P:(a + 1) * P], src[:, :, a * P:(a + 1) * P],
                                         repeat(const("mneg"), 2), ALU.add))
                p3 = att_s[n % 2].rearrange("p (h n) -> p h n", h=H)
                link(v.tensor_reduce(nmx[:, n % 2, 0:4], p3[:, :, 0:(a + 1) * P], AX, ALU.max))
                signal(v.tensor_scalar(nmx[:, n % 2, 0:4], nmx[:, n % 2, 0:4], -SCALE, None, ALU.mult),
                       att_max, n + 1)

            def weigh(i, name, first):
                z = zsum[:, i, :]
                link(v.reciprocal(z, z))
                z4 = z.rearrange("p (a h) -> p a h", a=NT)
                link(v.tensor_tensor(z4, z4, sgb[:, :, 768 + i:780:3], ALU.mult))
                dve.wait_ge(av_full, AV[name] + 1)
                o = obuf[:, NSA, :] if first else sqb
                signal(v.tensor_tensor(head_norm(o), head_norm(ps[:, 7, :]), bcast(z, HD), ALU.mult),
                       av_taken, AV[name] + 1)

            att_mask(0, 0)
            weigh(0, "cmp", True)
            att_mask(1, 1)
            att_mask(2, 0)
            dve.wait_ge(att_exp, 2)
            weigh(1, "sel", False)
            link(v.tensor_tensor(obuf[:, NSA, :], obuf[:, NSA, :], sqb, ALU.add))
            att_mask(3, 1)
            dve.wait_ge(att_exp, 4)
            weigh(2, "win", False)
            signal(v.tensor_tensor(obuf[:, NSA, :], obuf[:, NSA, :], sqb, ALU.add), o_ready, 4)

            dve.wait_ge(proj_done, N_PROJ + N_GATE)
            for u in range(16):
                m, k = ORDER[u // 4], 2 * (u % 4)
                dve.wait_ge(up_full, u + 1)
                g = gates[:, m, k:k + 2, :].rearrange("p k t -> p (k t)")
                if u < 4:
                    dst = merged[:, k:k + 2, :].rearrange("p k t -> p (k t)")
                else:
                    if u >= 7:
                        dve.wait_ge(up_add, u - 6)
                    dst = mtmp[:, u % 3, :]
                signal(v.tensor_tensor(dst, ps[:, (u + 1) % 2, :], g, ALU.mult), up_mul, u + 1)
            for u in range(4):
                dve.wait_ge(y_full, u + 1)
                c = slice(u * 256, (u + 1) * 256)
                signal(v.tensor_tensor(xres[:, :, c], xres[:, :, c],
                                       ps[:, (u + 1) % 2, :].rearrange("p (a n) -> p a n", a=NT), ALU.add),
                       y_taken, u + 1)
                for a in range(NT):
                    link(v.tensor_tensor_reduce(xs2[:, a, c], xres[:, a, c], xres[:, a, c], 1.0, 0.0, ALU.mult,
                                                ALU.add, zs[:, 24 + 4 * a + u:25 + 4 * a + u]))
            rms(1, xs2, zs, g2_sb, xn2T, xhi, xlo)
            for n in range(2 * GROUP):
                s, j = n // GROUP, n % GROUP
                dve.wait_ge(hi_ready, n + 1)
                v.tensor_tensor(wlo[:, s, j], uring[:, s, j], whi[:, s, j], ALU.subtract).then_inc(lo_first, 1)

            def top16(values, index, src, tmp):
                link(v.max(values[:, 0:8], src))
                link(v.max_index(index[:, 0:8], values[:, 0:8], src))
                link(v.match_replace(tmp, values[:, 0:8], src, GONE))
                link(v.max(values[:, 8:16], tmp))
                link(v.max_index(index[:, 8:16], values[:, 8:16], tmp))

            for a in range(NT):
                for c in range(16):
                    if c % 4 == 0:
                        dve.wait_ge(s_done, 4 * a + c // 4 + 1)
                    top16(v16[:, a, c, :], iu[:, a, c, :], s_sb[:, a, c, :], rep[:, 0, 0:NK])
            for a in range(NT):
                for h in range(PH):
                    link(v.tensor_tensor(cand.rearrange("p (i j) -> p i j", j=PK), bcast(v16[:, a, 2 * h, :], PK),
                                         repeat(v16[:, a, 2 * h + 1, :], PK), ALU.add))
                    top16(vals[:, a, h, :], pos[:, a, h, :], cand, rep[:, 1, :])
            link(v.tensor_tensor(vals[:, :, :, 1:PK], vals[:, :, :, 1:PK],
                                 vals[:, :, :, 0:1].to_broadcast([P, NT, PH, PK - 1]), ALU.subtract))
            signal(v.tensor_tensor(vals[:, :, :, 0:1], vals[:, :, :, 0:1], vals[:, :, :, 0:1], ALU.subtract),
                   vals_ready, 1)
            flat = lambda ap: ap.rearrange("p a c k -> p (a c k)")
            link(v.tensor_copy(flat(if_), flat(iu)))
            eq = rt_big.rearrange("p (c k j) -> p c k j", c=PH, k=PK)
            for w in range(2):
                if w == 0:
                    link(v.tensor_scalar(posr, flat(pos), 4, None, ALU.logical_shift_right))
                else:
                    link(v.tensor_scalar(posr, flat(pos), 15, None, ALU.bitwise_and))
                link(v.tensor_copy(posf, posr))
                for a in range(NT):
                    link(v.tensor_tensor(rt_big.rearrange("p (n j) -> p n j", j=PK),
                                         bcast(posf[:, a * 128:(a + 1) * 128], PK),
                                         repeat(const("iota16"), 128), ALU.is_equal))
                    link(v.tensor_tensor(eq, eq, repeat(if_[:, a, w::2, :], PK, axis=2), ALU.mult))
                    link(v.tensor_reduce(picked[:, w, a, :], rt_big.rearrange("p (n j) -> p n j", j=PK), AX,
                                         ALU.add))
            dve.wait_ge(g_exp, 1)
            z16 = zs[:, 8:24]
            v3 = vals.rearrange("p a c k -> p (a c) k")
            link(v.tensor_reduce(z16, v3, AX, ALU.add))
            link(v.reciprocal(z16, z16))
            signal(v.tensor_tensor(v3, v3, bcast(z16, PK), ALU.mult), routed, 1)
            dve.wait_ge(tr_full, TR["i"] + 1)
            link(v.tensor_copy(i1T, ps[:, 6, 0:T]))
            signal(v.tensor_copy(i2T, ps[:, 6, T:2 * T]), tr_taken, TR["i"] + 1)
            dve.wait_ge(tr_full, TR["g"] + 1)
            rounded = oh1[:, 0].rearrange("p t n -> p (t n)")[:, 0:T]
            link(v.tensor_copy(rounded, ps[:, 6, 0:T]))
            link(v.tensor_copy(ghT, rounded))
            signal(v.tensor_tensor(glT, ps[:, 6, 0:T], ghT, ALU.subtract), tr_taken, TR["g"] + 1)

            def one_hots(s, n, half, first=False):
                tokens, columns = bass.ds(n * TB, TB), slice(half * NJ, (half + 1) * NJ)
                if not first:
                    dve.wait_ge(oh_ready, n + half * NS)
                v.tensor_tensor(eq2, repeat(const("iota")[:, columns], TB), bcast(i2T[:, tokens], NJ), ALU.is_equal
                                ).then_inc(eq_ready, 1)
                v.tensor_tensor(oh1[:, s], repeat(const("iota"), TB), bcast(i1T[:, tokens], NK), ALU.is_equal)
                dve.wait_ge(eq_ready, n + half * NS + 1)
                v.tensor_tensor(oh2h[:, s], eq2, bcast(ghT[:, tokens], NJ), ALU.mult)
                v.tensor_tensor(oh2l[:, s], eq2, bcast(glT[:, tokens], NJ), ALU.mult).then_inc(oh_ready, 1)

            def times_g(s, n, half):
                dve.wait_ge(g_full, n + half * NS + 1)
                h_ = hbuf[:, half * NJ:(half + 1) * NJ, bass.ds(n * TB, TB)]
                v.tensor_tensor(h_, h_, ps[:, 6 + s, :].rearrange("p (t j) -> p j t", t=TB), ALU.mult
                                ).then_inc(g_taken, 1)

            one_hots(0, 0, 0, first=True)
            dve.wait_ge(gelu_done, NG // 2)
            with dve.Fori(0, NS // 2 - 1) as i:
                for s in range(2):
                    one_hots(1 - s, i * 2 + s + 1, 0)
                    times_g(s, i * 2 + s, 0)
            one_hots(1, NS - 1, 0)
            times_g(0, NS - 2, 0)
            one_hots(0, 0, 1)
            times_g(1, NS - 1, 0)

            def a_low(s, g):
                dve.wait_ge(ahi_ready, g + 1)
                v.tensor_tensor(alo[:, s % 2].rearrange("p j t -> p (j t)"),
                                hbuf[:, bass.ds(g * GROUP, GROUP), :].rearrange("p j t -> p (j t)"),
                                ahi[:, s % 2].rearrange("p j t -> p (j t)"), ALU.subtract
                                ).then_inc(alo_ready, 1)

            a_low(0, 0)
            a_low(1, 1)

            def v_step(i, s, spreads=False):
                g = i * 2 + s
                if spreads:
                    one_hots(1 - s, g + 1, 1)
                    times_g(s, g, 1)
                dve.wait_ge(group_full, g + NG + 1)
                a_low(s, g + 2)

            dve.wait_ge(gelu_done, NG)
            with dve.Fori(0, NS // 2 - 1) as i:
                for s in range(2):
                    v_step(i, s, spreads=True)
            one_hots(1, NS - 1, 1)
            times_g(0, NS - 2, 1)
            times_g(1, NS - 1, 1)
            v_step(NS // 2 - 1, 0)
            v_step(NS // 2 - 1, 1)
            with dve.Fori(NS // 2, NG // 2 - 1) as i:
                for s in range(2):
                    v_step(i, s)
            for a in range(NT):
                dve.wait_ge(y2_full, a + 1)
                v.tensor_tensor(xres[:, a, :].rearrange("p (c n) -> p c n", c=2),
                                xres[:, a, :].rearrange("p (c n) -> p c n", c=2),
                                ps[:, 2 + 2 * a:4 + 2 * a, :], ALU.add).then_inc(y2_ready, 1)

        @block.gpsimd
        def _(pool):
            g = nc.gpsimd
            def w_low(m):
                pool.wait_ge(whi_ready, SPLIT.index(m) + 1)
                g.tensor_tensor(wpart(m, 1), wslot(m), wpart(m, 0), ALU.subtract
                                ).then_inc(wlo_ready, 1)

            for m in SPLIT[:2]:
                w_low(m)
            pool.wait_ge(qk_normed, 1)
            cos4 = repeat(const("cos").rearrange("p (a n) -> p a n", a=NT), 16, axis=2)
            sin4 = repeat(const("sin").rearrange("p (a n) -> p a n", a=NT), 16, axis=2)
            g.tensor_copy(qn, tm[:, :, 512:768]).then_inc(qn_ready, 1)
            g.tensor_tensor(ropes[2], tmh[:, :, :, 0:32], sin4, ALU.mult).then_inc(rope_pool, 1)
            g.tensor_tensor(ropes[3], tmh[:, :, :, 32:64], cos4, ALU.mult).then_inc(rope_pool, 1)
            w_low(12)
            pool.wait_ge(roped, 2)
            for a in range(NT):
                g.tensor_copy(kdup[:, a], repeat(tmh[:, a, 12:16, :], 2, axis=2)).then_inc(kdup_ready, 1)
            w_low(14), w_low(15)
            pool.wait_ge(av_full, AV["hg"] + 1)
            pool.wait_ge(proj_done, 9)
            pool.wait_ge(params_loaded, 16)
            done = 0

            def one_by_one(ins):
                nonlocal done
                done += 1
                ins.then_inc(kcp_ready, 1)
                pool.wait_ge(kcp_ready, done)

            wait_low(pool, 15)
            for half in range(2):
                kc4 = kcp[half].rearrange("p (w g t) -> p w g t", w=2, g=2)
                for grp in range(2):
                    r, other = slice(64 * grp, 64 * grp + 64), slice(64 - 64 * grp, 128 - 64 * grp)
                    one_by_one(g.memset(kc4[other, :, grp, :], 0.0))
                    for w in range(2):
                        pe_ = par("pe")[r, w * CMPL + half * CMPS:w * CMPL + (half + 1) * CMPS]
                        one_by_one(g.tensor_tensor(kc4[r, w, grp, :].rearrange("p (n l) -> p n l", l=CMPS),
                                                   fm_c[r, w, :].rearrange("p (n l) -> p n l", l=CMPS),
                                                   repeat(pe_, T // CMPS), ALU.add))
            for m in SPLIT[5:]:
                w_low(m)
            for u in range(4, 16):
                k = 2 * (u % 4)
                pool.wait_ge(up_mul, u + 1)
                o = merged[:, k:k + 2, :].rearrange("p k t -> p (k t)")
                if u >= 8:
                    pool.wait_ge(up_add, u - 7)
                g.tensor_tensor(o, o, mtmp[:, u % 3, :], ALU.add).then_inc(up_add, 1)

            def low(s, at, hi_at):
                pool.wait_ge(u_loaded[s % 4], at)
                for j in range(GROUP):
                    pool.wait_ge(hi_ready, hi_at + j)
                    g.tensor_tensor(wlo[:, s % 2, j], uring[:, s % 4, j], whi[:, s % 2, j], ALU.subtract
                                    ).then_inc(lo_ready, 1)

            def step(i, s):
                l = i * 4 + s
                pool.wait_ge(group_full, l + 1)
                low(s + 2, i * 16 + (16 if s < 2 else 32), l * GROUP + 2 * GROUP + 1)

            with pool.Fori(0, NG // 2 - 1) as i:
                for s in range(4):
                    step(i, s)
            step(NG // 2 - 1, 0)
            step(NG // 2 - 1, 1)


def kernel(x, norm1_g, w_in, hgrn_lb, hgrn_onorm_g, mlstm_conv_w, mlstm_conv_b, mlstm_gate_b,
           mlstm_onorm_g, nsa_qnorm_g, nsa_knorm_g, nsa_cmp_pe, nsa_cmp_w, ret_onorm_g, w_up,
           w_gate, w_out, norm2_g, peer_wq, peer_keys, peer_u, peer_v):
    import numpy as np
    import concourse.bacc as bacc
    from concourse.bass_utils import run_bass_kernel_spmd

    f = np.float32
    arr = lambda a: np.asarray(a)[0]

    def tiles(w):
        return np.ascontiguousarray(w.reshape(-1, P, w.shape[1]).transpose(1, 0, 2))

    def slot(w):
        t = tiles(w).reshape(P, -1)
        return t

    col, at = {}, 0
    for name, n in WIDTHS.items():
        col[name] = (at, at + n)
        at += n
    wi = arr(w_in)
    a_in = np.zeros((len(PROJ), P, UNIT), wi.dtype)
    for s, names in enumerate(PROJ):
        part = slot(np.concatenate([np.zeros((D, n), wi.dtype) if isinstance(n, int) else
                                    wi[:, col[n][0]:col[n][1]] for n in names], axis=1))
        a_in[s, :, :part.shape[1]] = part
    wc = arr(nsa_cmp_w).reshape(2, CMPL, HD, HD).transpose(2, 1, 0, 3).reshape(HD, -1)
    a_cmp = np.concatenate([wc, wc], axis=0)
    wg = arr(w_gate)
    a_gate = np.stack([slot(wg[m][:, c * 256:(c + 1) * 256]) for m in ORDER for c in range(4)])
    wu = arr(w_up)
    a_up = np.stack([slot(wu[m]) for m in ORDER])
    wo = arr(w_out)
    a_out = np.stack([slot(wo[:, c * 256:(c + 1) * 256]) for c in range(4)])
    wqa = arr(peer_wq)
    a_wq = np.stack([slot(wqa[:, c * 256:(c + 1) * 256]) for c in range(8)])
    a_keys = np.ascontiguousarray(arr(peer_keys).reshape(16, NK, P).transpose(2, 0, 1).reshape(P, -1))
    ua = arr(peer_u).reshape(NK, NG, GROUP, KD, P)
    a_u = np.ascontiguousarray(ua.transpose(1, 4, 2, 3, 0)).reshape(NG, P, GROUP * D)
    va = arr(peer_v).reshape(NK, NG, GROUP, D)
    a_v = np.ascontiguousarray(va.transpose(1, 0, 2, 3)).reshape(NG, P, GROUP * D)

    i = np.arange(P)
    tri = (i[:, None] <= i[None, :]).astype(f)
    c = {}
    c["ident"] = np.eye(P, dtype=f)
    c["iota"] = np.broadcast_to(i.astype(f), (P, P))
    c["iota16"] = np.broadcast_to(np.arange(16, dtype=f), (P, 16))
    inv = 1.0 / (f(10000.0) ** (np.arange(0, HD, 2, dtype=f) / f(HD)))
    ang = (np.arange(T, dtype=f)[:, None] * inv[None, :].astype(f)).astype(f)
    by_tile = lambda t: t.reshape(NT, P, -1).transpose(1, 0, 2).reshape(P, -1).astype(f)
    c["cos"], c["sin"] = by_tile(np.cos(ang)), by_tile(np.sin(ang))
    c["mneg"] = np.where(tri.T > 0, 0.0, NEG).astype(f)
    c["c01"] = np.concatenate([tri, np.ones((P, P), f), tri], axis=1) * f(SCALE)
    lg = np.log1p(-np.exp2(-5.0 - np.arange(H)))
    diff = i[None, :] - i[:, None]
    retd = []
    for h in range(H):
        d0 = np.where(diff >= 0, np.exp(lg[h] * np.maximum(diff, 0)), 0.0)
        retd += [d0, np.exp(lg[h] * (diff + P)), d0]
    c["retd"] = (np.concatenate(retd, axis=1) * SCALE).astype(f)
    c["reset"] = np.broadcast_to((np.arange(T) % 64 != 0).astype(f), (P, T))
    c["ones"] = np.ones((P, T), f)
    blocks_end = np.arange(16) * CMPS + CMPL - 1
    ok = (blocks_end[None, :] <= np.arange(T)[:, None])
    ok[:, NCMP:] = False
    c["cmp01"] = by_tile(ok.astype(f))
    c["cmpneg"] = by_tile(np.where(ok, 0.0, NEG).astype(f))
    sel = np.zeros((P, H, P), f)
    for h in range(H):
        sel[h, h] = 1.0
    c["sel"] = sel.reshape(P, -1)
    lv = [np.eye(P, dtype=f)]
    for L in LEVELS[1:8]:
        b = i // (2 * L)
        lv.append(((b[:, None] == b[None, :]) & ((i % (2 * L) < L)[:, None]) & ((i % (2 * L) >= L)[None, :])
                   ).astype(f))
    c["level"] = np.concatenate(lv, axis=1)
    pack = lambda table, src: np.ascontiguousarray(np.concatenate([src[n].reshape(P, -1) for n in table], axis=1))
    a_late, a_front = pack(CONST_LATE, c).astype(f), pack(CONST_FRONT, c).astype(f)

    rep = lambda a: np.broadcast_to(a.reshape(1, -1), (P, a.size))
    p = {}
    p["g1"] = arr(norm1_g).reshape(KD, P).T
    cwa = arr(mlstm_conv_w)
    p["cw"] = cwa.reshape(4, 4, P).transpose(2, 1, 0).reshape(P, 16)
    p["cb"] = arr(mlstm_conv_b).reshape(4, P).T
    pea = arr(nsa_cmp_pe).transpose(2, 0, 1).reshape(HD, 2 * CMPL)
    p["pe"] = np.concatenate([pea, pea], axis=0)
    gb = np.zeros((P, 2), f)
    gb[0:4] = arr(mlstm_gate_b).reshape(2, 4).T
    p["gb"] = gb
    p["gh"], p["gm"], p["gr"] = rep(arr(hgrn_onorm_g)), rep(arr(mlstm_onorm_g)), rep(arr(ret_onorm_g))
    qn, kn = arr(nsa_qnorm_g), arr(nsa_knorm_g)
    p["gqk"] = rep(np.concatenate([qn] * 4 + [kn[1]] * 2 + [kn[2]] * 2))
    p["gkc"] = rep(np.concatenate([kn[0]] * 2))
    a_par = pack(PARAMS, p)
    a_g2 = np.ascontiguousarray(arr(norm2_g).reshape(KD, P).T)
    a_x = np.ascontiguousarray(arr(x).reshape(NT, P, D).transpose(1, 0, 2))

    arrays = dict(x=a_x, w_in=a_in, w_cmp=np.ascontiguousarray(a_cmp), w_gate=a_gate,
                  w_up=a_up, w_out=a_out, wq=a_wq, keys=a_keys, u_tab=a_u, v_tab=a_v, g2=a_g2,
                  late=a_late, front=a_front, params=a_par)
    nc = bacc.Bacc("TRN2", target_bir_lowering=False, num_devices=1)
    args = [nc.dram_tensor(f"in_{n}", a.shape, mybir.dt.from_np(a.dtype), kind="ExternalInput").ap()
            for n, a in arrays.items()]
    out = nc.dram_tensor("out", (T, D), F32, kind="ExternalOutput").ap()
    build(nc, *args, out)
    r = run_bass_kernel_spmd(nc, [{f"in_{n}": a for n, a in arrays.items()}], core_ids=[0])
    return r.results[0]["out"].reshape(1, T, D)
```
